# Optimizing a Trainium2 kernel written in Bass

```python
import math
import jax, jax.numpy as jnp
from jax import lax
import numpy as np

D_MODEL = 1024
BATCH = 1
SEQ = 2048
DEPTH = 1

N_META = 16
MLA_HEADS = 4
QK_NOPE_DIM = 128
QK_ROPE_DIM = 64
QK_HEAD_DIM = QK_NOPE_DIM + QK_ROPE_DIM
V_HEAD_DIM = 128
Q_LORA_RANK = 256
KV_LORA_RANK = 256
ROPE_THETA = 10000.0
Q_BLOCK = 128
DN_HEADS = 4
DN_HEAD_DIM = 128
DN_WIDTH = DN_HEADS * DN_HEAD_DIM
DN_CONV_WIDTH = 4
DN_CHUNK = 64
MIX_WIDTH = MLA_HEADS * V_HEAD_DIM + DN_WIDTH
IN_COLS = Q_LORA_RANK + KV_LORA_RANK + QK_ROPE_DIM + 3 * DN_WIDTH + DN_WIDTH + 2 * DN_HEADS
D_FF = 2816
FFN_CONV_WIDTH = 3
NORM_EPS = 1e-6

kernel_name = "hymba_mla_gdn_convglu_layer"

def _rmsnorm(x, w):
    xf = x.astype(jnp.float32)
    y = xf * lax.rsqrt(jnp.mean(xf * xf, axis=-1, keepdims=True) + NORM_EPS)
    return (y * w.astype(jnp.float32)).astype(x.dtype)

def _l2norm(x):
    return x * lax.rsqrt(jnp.sum(x * x, axis=-1, keepdims=True) + NORM_EPS)

def _causal_dwconv(x, w):
    width, channels = w.shape
    return lax.conv_general_dilated(
        x, w[:, None, :].astype(x.dtype), window_strides=(1,),
        padding=[(width - 1, 0)], dimension_numbers=("NWC", "WIO", "NWC"),
        feature_group_count=channels)

def _rope(x, pos):
    half = x.shape[-1] // 2
    inv_freq = ROPE_THETA ** (-jnp.arange(half, dtype=jnp.float32) / half)
    ang = pos.astype(jnp.float32)[:, None] * inv_freq[None, :]
    cos = jnp.cos(ang)[None, :, None, :]
    sin = jnp.sin(ang)[None, :, None, :]
    xf = x.astype(jnp.float32)
    x1, x2 = xf[..., :half], xf[..., half:]
    return jnp.concatenate([x1 * cos - x2 * sin, x1 * sin + x2 * cos], axis=-1).astype(x.dtype)

def _causal_attention(q, k, v):
    B, H, L, dq = q.shape
    dv = v.shape[-1]
    nb = -(-L // Q_BLOCK)
    Lp = nb * Q_BLOCK
    pad = ((0, 0), (0, 0), (0, Lp - L), (0, 0))
    q, k, v = jnp.pad(q, pad), jnp.pad(k, pad), jnp.pad(v, pad)
    scale = 1.0 / math.sqrt(dq)
    q_blocks = q.reshape(B, H, nb, Q_BLOCK, dq).transpose(2, 0, 1, 3, 4)
    key_pos = jnp.arange(Lp)

    def one_block(args):
        qb, start = args
        s = jnp.einsum("bhqd,bhkd->bhqk", qb, k).astype(jnp.float32) * scale
        q_pos = start + jnp.arange(Q_BLOCK)
        mask = key_pos[None, :] <= q_pos[:, None]
        p = jax.nn.softmax(jnp.where(mask, s, -jnp.inf), axis=-1)
        return jnp.einsum("bhqk,bhkd->bhqd", p.astype(v.dtype), v)

    out = lax.map(one_block, (q_blocks, jnp.arange(nb) * Q_BLOCK))
    return out.transpose(1, 2, 0, 3, 4).reshape(B, H, Lp, dv)[:, :, :L]

def _mla(q_lat, kv_lat, k_pe, pos, q_a_norm_w, w_q_b, kv_a_norm_w, w_kv_b,
         q_norm_w, k_norm_w, mla_out_norm_w):
    B, L, _ = q_lat.shape
    q = (_rmsnorm(q_lat, q_a_norm_w) @ w_q_b).reshape(B, L, MLA_HEADS, QK_HEAD_DIM)
    kv = (_rmsnorm(kv_lat, kv_a_norm_w) @ w_kv_b).reshape(B, L, MLA_HEADS, QK_NOPE_DIM + V_HEAD_DIM)
    k_nope, v = kv[..., :QK_NOPE_DIM], kv[..., QK_NOPE_DIM:]
    k = jnp.concatenate(
        [k_nope, jnp.broadcast_to(k_pe[:, :, None, :], (B, L, MLA_HEADS, QK_ROPE_DIM))], axis=-1)
    q = _rmsnorm(q, q_norm_w)
    k = _rmsnorm(k, k_norm_w)
    q = jnp.concatenate([q[..., :QK_NOPE_DIM], _rope(q[..., QK_NOPE_DIM:], pos)], axis=-1)
    k = jnp.concatenate([k[..., :QK_NOPE_DIM], _rope(k[..., QK_NOPE_DIM:], pos)], axis=-1)
    o = _causal_attention(q.transpose(0, 2, 1, 3), k.transpose(0, 2, 1, 3), v.transpose(0, 2, 1, 3))
    o = _rmsnorm(o.transpose(0, 2, 1, 3), mla_out_norm_w)
    return o.reshape(B, L, MLA_HEADS * V_HEAD_DIM)

def _chunk_gated_delta_rule(q, k, v, g, beta):
    B, H, T, dk = q.shape
    dv = v.shape[-1]
    C = DN_CHUNK
    N = T // C
    q = q * (1.0 / math.sqrt(dk))
    q = q.reshape(B, H, N, C, dk)
    k = k.reshape(B, H, N, C, dk)
    v = v.reshape(B, H, N, C, dv)
    g = jnp.cumsum(g.reshape(B, H, N, C), axis=-1)
    beta = beta.reshape(B, H, N, C)
    tri = jnp.tril(jnp.ones((C, C), dtype=bool))
    strict = jnp.tril(jnp.ones((C, C), dtype=jnp.float32), -1)
    decay = jnp.exp(jnp.where(tri, g[..., :, None] - g[..., None, :], -jnp.inf))
    k_beta = k * beta[..., None]
    v_beta = v * beta[..., None]
    a_strict = jnp.einsum("bhnid,bhnjd->bhnij", k_beta, k) * decay * strict
    eye = jnp.eye(C, dtype=jnp.float32)
    t_inv = lax.linalg.triangular_solve(
        eye + a_strict, jnp.broadcast_to(eye, a_strict.shape),
        left_side=True, lower=True, unit_diagonal=True)
    u = jnp.einsum("bhnij,bhnjd->bhnid", t_inv, v_beta)
    w = jnp.einsum("bhnij,bhnjd->bhnid", t_inv, k_beta * jnp.exp(g)[..., None])
    qk = jnp.einsum("bhnid,bhnjd->bhnij", q, k) * decay

    def step(S, inp):
        q_c, k_c, u_c, w_c, g_c, qk_c = inp
        v_new = u_c - jnp.einsum("bhcd,bhde->bhce", w_c, S)
        o = (jnp.einsum("bhcd,bhde->bhce", q_c * jnp.exp(g_c)[..., None], S)
             + jnp.einsum("bhij,bhje->bhie", qk_c, v_new))
        g_last = g_c[..., -1]
        S = (S * jnp.exp(g_last)[..., None, None]
             + jnp.einsum("bhcd,bhce->bhde", k_c * jnp.exp(g_last[..., None] - g_c)[..., None], v_new))
        return S, o

    to_scan = lambda t: jnp.moveaxis(t, 2, 0)
    S0 = jnp.zeros((B, H, dk, dv), jnp.float32)
    _, o = lax.scan(step, S0, (to_scan(q), to_scan(k), to_scan(u), to_scan(w), to_scan(g), to_scan(qk)))
    return jnp.moveaxis(o, 0, 2).reshape(B, H, T, dv)

def _gated_deltanet(qkv, z, a, b, dn_conv_w, dn_A_log, dn_dt_bias, dn_out_norm_w):
    B, L, _ = qkv.shape
    qkv = jax.nn.silu(_causal_dwconv(qkv, dn_conv_w)).astype(jnp.float32)
    heads = lambda t: t.reshape(B, L, DN_HEADS, DN_HEAD_DIM).transpose(0, 2, 1, 3)
    q = _l2norm(heads(qkv[..., :DN_WIDTH]))
    k = _l2norm(heads(qkv[..., DN_WIDTH:2 * DN_WIDTH]))
    v = heads(qkv[..., 2 * DN_WIDTH:])
    beta = jax.nn.sigmoid(b.astype(jnp.float32)).transpose(0, 2, 1)
    g = (-jnp.exp(dn_A_log.astype(jnp.float32))
         * jax.nn.softplus(a.astype(jnp.float32) + dn_dt_bias.astype(jnp.float32))).transpose(0, 2, 1)
    pad = (-N_META) % DN_CHUNK
    p4 = ((0, 0), (0, 0), (pad, 0), (0, 0))
    p3 = ((0, 0), (0, 0), (pad, 0))
    o = _chunk_gated_delta_rule(jnp.pad(q, p4), jnp.pad(k, p4), jnp.pad(v, p4),
                                jnp.pad(g, p3), jnp.pad(beta, p3))[:, :, pad:]
    o = _rmsnorm(o.transpose(0, 2, 1, 3), dn_out_norm_w)
    o = o * jax.nn.silu(z.reshape(B, L, DN_HEADS, DN_HEAD_DIM).astype(jnp.float32))
    return o.reshape(B, L, DN_WIDTH).astype(qkv.dtype if False else z.dtype)

def _conv_glu(h, w_gate, w_up, ffn_conv_w, ffn_conv_b, w_down):
    gate = _causal_dwconv(h @ w_gate, ffn_conv_w) + ffn_conv_b
    return (jax.nn.silu(gate) * (h @ w_up)) @ w_down

def setup_inputs(seed: int = 0) -> dict:
    key = jax.random.key(seed)
    ks = jax.random.split(key, 26)
    f32 = jnp.float32
    nrm = lambda k, shape, scale: jax.random.normal(k, shape, f32) * scale
    gain = lambda k, shape: 1.0 + 0.02 * jax.random.normal(k, shape, f32)
    Ld = DEPTH
    dt = jnp.exp(jax.random.uniform(ks[14], (Ld, DN_HEADS), f32, math.log(1e-3), math.log(1e-1)))
    return {
        "x": nrm(ks[0], (BATCH, SEQ, D_MODEL), 1.0),
        "meta_tokens": nrm(ks[1], (N_META, D_MODEL), 1.0),
        "attn_norm_w": gain(ks[2], (Ld, D_MODEL)),
        "w_in": nrm(ks[3], (Ld, D_MODEL, IN_COLS), D_MODEL ** -0.5),
        "q_a_norm_w": gain(ks[4], (Ld, Q_LORA_RANK)),
        "w_q_b": nrm(ks[5], (Ld, Q_LORA_RANK, MLA_HEADS * QK_HEAD_DIM), Q_LORA_RANK ** -0.5),
        "kv_a_norm_w": gain(ks[6], (Ld, KV_LORA_RANK)),
        "w_kv_b": nrm(ks[7], (Ld, KV_LORA_RANK, MLA_HEADS * (QK_NOPE_DIM + V_HEAD_DIM)), KV_LORA_RANK ** -0.5),
        "q_norm_w": gain(ks[8], (Ld, QK_HEAD_DIM)),
        "k_norm_w": gain(ks[9], (Ld, QK_HEAD_DIM)),
        "mla_out_norm_w": gain(ks[10], (Ld, V_HEAD_DIM)),
        "dn_conv_w": nrm(ks[11], (Ld, DN_CONV_WIDTH, 3 * DN_WIDTH), DN_CONV_WIDTH ** -0.5),
        "dn_A_log": jnp.log(jax.random.uniform(ks[12], (Ld, DN_HEADS), f32, 1.0, 16.0)),
        "dn_dt_bias": dt + jnp.log(-jnp.expm1(-dt)),
        "dn_out_norm_w": gain(ks[13], (Ld, DN_HEAD_DIM)),
        "w_out": nrm(ks[15], (Ld, MIX_WIDTH, D_MODEL), MIX_WIDTH ** -0.5),
        "ffn_norm_w": gain(ks[16], (Ld, D_MODEL)),
        "w_gate": nrm(ks[17], (Ld, D_MODEL, D_FF), D_MODEL ** -0.5),
        "w_up": nrm(ks[18], (Ld, D_MODEL, D_FF), D_MODEL ** -0.5),
        "ffn_conv_w": nrm(ks[19], (Ld, FFN_CONV_WIDTH, D_FF), FFN_CONV_WIDTH ** -0.5),
        "ffn_conv_b": nrm(ks[20], (Ld, D_FF), 0.01),
        "w_down": nrm(ks[21], (Ld, D_FF, D_MODEL), D_FF ** -0.5),
    }

def reference(x, meta_tokens, attn_norm_w, w_in, q_a_norm_w, w_q_b, kv_a_norm_w, w_kv_b,
              q_norm_w, k_norm_w, mla_out_norm_w, dn_conv_w, dn_A_log, dn_dt_bias,
              dn_out_norm_w, w_out, ffn_norm_w, w_gate, w_up, ffn_conv_w, ffn_conv_b, w_down):
    B = x.shape[0]
    meta = jnp.broadcast_to(meta_tokens[None].astype(x.dtype), (B, N_META, D_MODEL))
    h = jnp.concatenate([meta, x], axis=1)
    L = h.shape[1]
    pos = jnp.arange(L, dtype=jnp.int32)
    c1 = Q_LORA_RANK
    c2 = c1 + KV_LORA_RANK
    c3 = c2 + QK_ROPE_DIM
    c4 = c3 + 3 * DN_WIDTH
    c5 = c4 + DN_WIDTH
    c6 = c5 + DN_HEADS
    for l in range(DEPTH):
        u = _rmsnorm(h, attn_norm_w[l])
        proj = u @ w_in[l]
        q_lat, kv_lat, k_pe = proj[..., :c1], proj[..., c1:c2], proj[..., c2:c3]
        dn_qkv, dn_z = proj[..., c3:c4], proj[..., c4:c5]
        dn_a, dn_b = proj[..., c5:c6], proj[..., c6:]
        y_mla = _mla(q_lat, kv_lat, k_pe, pos, q_a_norm_w[l], w_q_b[l], kv_a_norm_w[l], w_kv_b[l],
                     q_norm_w[l], k_norm_w[l], mla_out_norm_w[l])
        y_dn = _gated_deltanet(dn_qkv, dn_z, dn_a, dn_b, dn_conv_w[l], dn_A_log[l], dn_dt_bias[l],
                               dn_out_norm_w[l])
        mixed = jnp.concatenate([y_mla, y_dn], axis=-1)
        h = h + mixed @ w_out[l]
        h = h + _conv_glu(_rmsnorm(h, ffn_norm_w[l]), w_gate[l], w_up[l], ffn_conv_w[l],
                          ffn_conv_b[l], w_down[l])
    return h[:, N_META:]


_drawn_inputs = setup_inputs


def setup_inputs(seed=0):
    import zlib

    import numpy as np

    out = dict(_drawn_inputs(seed))
    spreads = {}
    factors = {'q_a_norm_w': 4.972,
     'kv_a_norm_w': 2.909,
     'q_norm_w': 4.541,
     'k_norm_w': 4.69,
     'mla_out_norm_w': 11.256,
     'dn_out_norm_w': 21.721,
     'ffn_norm_w': 4.694,
     'ffn_conv_b': 27.318}
    for name, (base, spread) in spreads.items():
        noise = np.random.default_rng([zlib.crc32(name.encode()), seed]).standard_normal(out[name].shape)
        drawn = base * np.exp(spread * noise) if base else spread * noise
        out[name] = __import__('jax').numpy.asarray(drawn.astype(out[name].dtype))
    for name, factor in factors.items():
        out[name] = (out[name] * factor).astype(out[name].dtype)
    return out
```

```python
from contextlib import ExitStack

import numpy as np
import concourse.bass as bass
from concourse import mybir

F32 = mybir.dt.float32
F32R = mybir.dt.float32r
ALU = mybir.AluOpType
ACT = mybir.ActivationFunctionType
AX = mybir.AxisListType

P = 128
SEQ = 2048
N_META = 16
L = N_META + SEQ
TILES = -(-L // P)
LP = TILES * P
D = 1024
KD = D // P
HEADS = 4
NOPE, ROPE, VD = 128, 64, 128
QK = NOPE + ROPE
HALF = ROPE // 2
LORA = 256
DNW = 512
CHUNK = 64
DN_PAD = (-N_META) % CHUNK
CHUNKS = (DN_PAD + L) // CHUNK
C_KPE = 2 * LORA
C_QKV = C_KPE + ROPE
C_Z = C_QKV + 3 * DNW
C_AB = C_Z + DNW
TOKW = 2 * LORA + DNW + ROPE + 2 * HEADS
D_FF = 2816
FT = D_FF // P
EPS = 1e-6


def tiles(eng, n, front, mid, back=None):
    def at(t):
        return (t, t % 2, t // 2)

    def step(t, nxt, prev):
        if nxt is not None and front:
            front(*nxt)
        if mid:
            mid(*t)
        if prev is not None and back:
            back(*prev)

    if front:
        front(*at(0))
    step(at(0), at(1), None)
    turns = (n - 2) // 2
    with eng.Fori(0, turns) as p:
        even, odd, even2, odd2 = (2 * p, 0, p), (2 * p + 1, 1, p), (2 * p + 2, 0, p + 1), (2 * p + 3, 1, p + 1)
        step(odd, even2, even)
        step(even2, odd2, odd)
    for t in range(2 * turns + 1, n):
        step(at(t), at(t + 1) if t + 1 < n else None, at(t - 1))
    if back:
        back(*at(n - 1))


class Room:

    def __init__(self, nc, ctx, stage):
        self.nc, self.ctx, self.stage = nc, ctx, stage

    def sb(self, name, shape, dt=F32):
        return self.ctx.enter_context(self.nc.sbuf_tensor(f"{self.stage}_{name}", shape, dt))

    def ps(self, name, shape, dt=F32):
        return self.ctx.enter_context(self.nc.psum_tensor(f"{self.stage}_{name}", shape, dt))

    def sem(self, name):
        return self.nc.alloc_semaphore(f"{self.stage}_{name}")

    def sems(self, name, n=2):
        return [self.sem(f"{name}{i}") for i in range(n)]


def f(ap):
    return ap.bitcast(F32)


def make_identity(pool, ident, made):
    pool.memset(ident[:, :], 0.0).then_inc(made, 1)
    pool.wait_ge(made, 1)
    pool.affine_select(out=ident[:, :], in_=ident[:, :], compare_op=ALU.not_equal, fill=1.0, base=0,
                       pattern=[[-1, P]], channel_multiplier=1).then_inc(made, 1)


def stage_project(nc, A, S):
    with ExitStack() as ctx:
        r = Room(nc, ctx, "pj")
        w_hi = r.sb("w_hi", [P, KD, TOKW], F32R)
        w_lo = r.sb("w_lo", [P, KD, TOKW], F32R)
        w_raw = [r.sb(f"w_raw{i}", [P, TOKW]) for i in range(2)]
        gain = r.sb("gain", [P, D])
        ident = r.sb("ident", [P, P])
        eps = r.sb("eps", [P, 1])
        xt = [r.sb(f"xt{i}", [P, D]) for i in range(2)]
        xn = [r.sb(f"xn{i}", [P, D]) for i in range(2)]
        u_hi = [r.sb(f"u_hi{i}", [P, KD, P], F32R) for i in range(2)]
        u_lo = [r.sb(f"u_lo{i}", [P, KD, P], F32R) for i in range(2)]
        tok = [r.sb(f"tok{i}", [P, TOKW]) for i in range(2)]
        junk = r.sb("junk", [P, D])
        ss = [r.sb(f"ss{i}", [P, 4]) for i in range(2)]
        pT = r.ps("pT", [P, KD, P])
        pP = [r.ps(f"pP{i}", [P, 3, 512]) for i in range(2)]

        w_loaded, w_half, w_ready = r.sems("w_loaded"), r.sem("w_half"), r.sem("w_ready")
        consts, id_made, head_loaded = r.sem("consts"), r.sem("id_made"), r.sem("head_loaded")
        x_loaded, x_sum, x_root, x_inv = r.sems("x_loaded"), r.sems("x_sum"), r.sems("x_root"), r.sems("x_inv")
        xn_ready, turned, hi_ready, u_ready = r.sems("xn_ready"), r.sems("turned"), r.sems("hi_ready"), r.sem("u_ready")
        projected, tok_ready = r.sems("projected"), r.sems("tok_ready")
        u_stored, tok_stored = r.sems("u_stored"), r.sems("tok_stored")

        block = ctx.enter_context(nc.Block())

        @block.sync
        def _(sp):
            sp.dma_start(gain[:, :], A["attn_norm_w"][0:1, :].to_broadcast([P, D])).then_inc(consts, 16)

            def load(t, s, u):
                sp.wait_ge(xn_ready[s], u)
                if isinstance(t, int) and t == 0:
                    sp.dma_start(xt[0][0:N_META, :], A["meta_tokens"]).then_inc(head_loaded, 16)
                    sp.dma_start(xt[0][N_META:P, :], A["x"][0, 0:P - N_META, :]).then_inc(x_loaded[0], 16)
                elif isinstance(t, int) and t == TILES - 1:
                    sp.dma_start(xt[s][0:L % P, :], A["x"][0, SEQ - L % P:SEQ, :]).then_inc(x_loaded[s], 16)
                else:
                    sp.dma_start(xt[s][:, :], A["x"][0, bass.ds(t * P - N_META, P), :]).then_inc(x_loaded[s], 16)

            def weights():
                for k in range(KD):
                    if k >= 2:
                        sp.wait_ge(w_ready, k - 1)
                    rows = slice(k * P, k * P + P)
                    w = A["w_in"][0, rows, :]
                    for to, of, n in ((0, 0, 2 * LORA), (2 * LORA, C_Z, DNW), (2 * LORA + DNW, C_KPE, ROPE),
                                      (2 * LORA + DNW + ROPE, C_AB, 2 * HEADS)):
                        sp.dma_start(w_raw[k % 2][:, to:to + n], w[:, of:of + n]).then_inc(w_loaded[k % 2], 16)

            load(0, 0, 0)
            weights()
            first = [True]

            def front(t, s, u):
                if first[0]:
                    first[0] = False
                    return
                load(t, s, u)
            tiles(sp, TILES, front, None)

        @block.gpsimd
        def _(pool):
            make_identity(pool, ident, id_made)

            def store(t, s, u):
                cols = bass.ds(t * P, P)
                pool.wait_ge(u_ready, t + 1)
                pool.dma_start(S["uT"][0, :, :, cols], f(u_hi[s][:, :, :])).then_inc(u_stored[s], 16)
                pool.dma_start(S["uT"][1, :, :, cols], f(u_lo[s][:, :, :])).then_inc(u_stored[s], 16)
                pool.wait_ge(tok_ready[s], u + 1)
                pool.dma_start(S["tok"][cols, :], tok[s][:, :]).then_inc(tok_stored[s], 16)

            tiles(pool, TILES, None, store)
            for s in range(2):
                pool.wait_ge(u_stored[s], 32 * ((TILES + 1 - s) // 2))
                pool.wait_ge(tok_stored[s], 16 * ((TILES + 1 - s) // 2))

        @block.scalar
        def _(act):
            def split(k):
                act.wait_ge(w_loaded[k % 2], 64 * (k // 2 + 1))
                act.activation(w_hi[:, k, :], w_raw[k % 2][:, :], ACT.Copy).then_inc(w_half, 1)

            def front(t, s, u):
                if isinstance(t, int) and t == 0:
                    act.wait_ge(head_loaded, 16)
                    act.wait_ge(consts, 17)
                act.wait_ge(x_loaded[s], 16 * (u + 1))
                act.activation(junk[:, :], xt[s][:, :], ACT.Square, accum_out=ss[s][:, 0:1]).then_inc(x_sum[s], 1)
                act.wait_ge(x_sum[s], u + 1)
                act.activation(ss[s][:, 1:2], ss[s][:, 0:1], ACT.Sqrt, bias=eps[:, :],
                               scale=1.0 / D).then_inc(x_root[s], 1)
                if isinstance(t, int) and t == 0:
                    for k in range(KD):
                        split(k)

            def mid(t, s, u):
                act.wait_ge(turned[s], u + 1)
                act.wait_ge(u_stored[s], 32 * u)
                act.activation(u_hi[s][:, :, :], pT[:, :, :], ACT.Copy).then_inc(hi_ready[s], 1)

            def back(t, s, u):
                act.wait_ge(projected[s], u + 1)
                act.wait_ge(tok_stored[s], 16 * u)
                act.activation(tok[s][:, 0:1024].rearrange("p (b n) -> p b n", b=2), pP[s][:, 0:2, :], ACT.Copy)
                act.activation(tok[s][:, 1024:TOKW], pP[s][:, 2, 0:TOKW - 1024], ACT.Copy).then_inc(tok_ready[s], 1)

            tiles(act, TILES, front, mid, back)

        @block.vector
        def _(dve):
            dve.memset(eps[:, :], EPS).then_inc(consts, 1)
            dve.wait_ge(consts, 17)

            def front(t, s, u):
                dve.wait_ge(x_root[s], u + 1)
                dve.reciprocal(ss[s][:, 2:3], ss[s][:, 1:2]).then_inc(x_inv[s], 1)
                dve.wait_ge(x_inv[s], u + 1)
                dve.wait_ge(turned[s], u)
                dve.scalar_tensor_tensor(out=xn[s][:, :], in0=xt[s][:, :], scalar=ss[s][:, 2:3], in1=gain[:, :],
                                         op0=ALU.mult, op1=ALU.mult).then_inc(xn_ready[s], 1)
                if isinstance(t, int) and t == 0:
                    for k in range(KD):
                        dve.wait_ge(w_half, k + 1)
                        dve.tensor_tensor(w_lo[:, k, :], w_raw[k % 2][:, :], f(w_hi[:, k, :]),
                                          ALU.subtract).then_inc(w_ready, 1)

            def mid(t, s, u):
                dve.wait_ge(hi_ready[s], u + 1)
                dve.wait_ge(projected[s], u)
                dve.tensor_tensor(u_lo[s][:, :, :], pT[:, :, :], f(u_hi[s][:, :, :]), ALU.subtract).then_inc(u_ready, 1)

            tiles(dve, TILES, front, mid)

        @block.tensor
        def _(pe):
            pe.wait_ge(id_made, 2)

            def turn(t, s, u):
                pe.wait_ge(xn_ready[s], u + 1)
                pe.wait_ge(u_ready, t)
                for k in range(KD):
                    m = pe.transpose(pT[:, k, :], xn[s][:, k * P:k * P + P], ident[:, :])
                m.then_inc(turned[s], 1)

            def multiply(t, s, u):
                if isinstance(t, int) and t == 0:
                    pe.wait_ge(w_ready, KD)
                pe.wait_ge(u_ready, t + 1)
                pe.wait_ge(tok_ready[s], u)
                for bank, lo, n in ((0, 0, 512), (1, 512, 512), (2, 1024, TOKW - 1024)):
                    for k in range(KD):
                        for n_pass, (a, b) in enumerate(((u_hi, w_hi), (u_hi, w_lo), (u_lo, w_hi))):
                            m = pe.matmul(pP[s][:, bank, 0:n], a[s][:, k, :], b[:, k, lo:lo + n],
                                          start=(k == 0 and n_pass == 0), stop=(k == KD - 1 and n_pass == 2))
                m.then_inc(projected[s], 1)

            tiles(pe, TILES, None, turn, multiply)


def stage_qkv(nc, A, S):
    with ExitStack() as ctx:
        r = Room(nc, ctx, "qkv")
        QW, KVW = HEADS * QK, HEADS * (NOPE + VD)
        w_raw = r.sb("w_raw", [P, 2, QW + KVW])
        w_hi = r.sb("w_hi", [P, 2, QW + KVW], F32R)
        w_lo = r.sb("w_lo", [P, 2, QW + KVW], F32R)
        ident = r.sb("ident", [P, P])
        eps = r.sb("eps", [P, 1])
        lat_gain = r.sb("lat_gain", [P, 2 * LORA])
        nope_gain = r.sb("nope_gain", [P, 2])
        rope_gain = r.sb("rope_gain", [P, 2, ROPE])
        lat = [r.sb(f"lat{i}", [P, 2 * LORA]) for i in range(2)]
        kpe = [r.sb(f"kpe{i}", [P, ROPE]) for i in range(2)]
        trig = [r.sb(f"trig{i}", [P, 2, HALF]) for i in range(2)]
        latn = [r.sb(f"latn{i}", [P, 2 * LORA]) for i in range(2)]
        l_hi = [r.sb(f"l_hi{i}", [P, 4, P], F32R) for i in range(2)]
        l_lo = [r.sb(f"l_lo{i}", [P, 4, P], F32R) for i in range(2)]
        st = [r.sb(f"st{i}", [P, 8]) for i in range(2)]
        hs = [r.sb(f"hs{i}", [P, 3, 8]) for i in range(2)]
        q = [r.sb(f"q{i}", [P, HEADS, QK]) for i in range(2)]
        kv = [r.sb(f"kv{i}", [P, HEADS, NOPE + VD]) for i in range(2)]
        qn = [r.sb(f"qn{i}", [P, HEADS, QK]) for i in range(2)]
        kn = [r.sb(f"kn{i}", [P, HEADS, NOPE]) for i in range(2)]
        qg = r.sb("qg", [P, HEADS, ROPE])
        kg = r.sb("kg", [P, ROPE])
        qprod = r.sb("qprod", [P, 4, HEADS, HALF])
        kprod = r.sb("kprod", [P, 4, HALF])
        kturn = r.sb("kturn", [P, ROPE])
        qrope = [r.sb(f"qrope{i}", [P, HEADS, ROPE]) for i in range(2)]
        krope = [r.sb(f"krope{i}", [P, HEADS, ROPE]) for i in range(2)]
        qx = [r.sb(f"qx{i}", [P, 6, P]) for i in range(2)]
        kx = [r.sb(f"kx{i}", [P, 6, P]) for i in range(2)]
        junk = r.sb("junk", [P, QW])
        junk_l = r.sb("junk_l", [P, 2 * LORA + ROPE])
        junk_k = r.sb("junk_k", [P, HEADS, NOPE])
        pL = r.ps("pL", [P, 4, P])
        pQ = r.ps("pQ", [P, 1024])
        pKV = r.ps("pKV", [P, 1024])
        pX = r.ps("pX", [P, 3, 4, P])

        consts, id_made, w_loaded = r.sem("consts"), r.sem("id_made"), r.sem("w_loaded")
        w_half, w_ready = r.sem("w_half"), r.sem("w_ready")
        loaded, lat_sum, lat_root, lat_inv = r.sems("loaded"), r.sems("lat_sum"), r.sems("lat_root"), r.sems("lat_inv")
        latn_ready, lat_turned, l_hi_ready, l_ready = r.sems("latn_ready"), r.sems("lat_turned"), r.sems("l_hi_ready"), r.sems("l_ready")
        multiplied, q_out, kv_out = r.sems("multiplied"), r.sems("q_out"), r.sems("kv_out")
        squares, sums, sums_all, roots, inverses = r.sems("squares"), r.sems("sums"), r.sems("sums_all"), r.sems("roots"), r.sems("inverses")
        scaled, pool_step, q_rotated, k_turned, k_rotated = r.sems("scaled"), r.sem("pool_step"), r.sems("q_rotated"), r.sems("k_turned"), r.sems("k_rotated")
        turned, qx_ready, kx_ready, stored, v_stored = r.sems("turned"), r.sems("qx_ready"), r.sems("kx_ready"), r.sems("stored"), r.sems("v_stored")

        block = ctx.enter_context(nc.Block())

        @block.sync
        def _(sp):
            sp.dma_start(w_raw[:, :, 0:QW], A["w_q_b"][0].rearrange("(k p) n -> p k n", p=P)).then_inc(w_loaded, 16)
            sp.dma_start(w_raw[:, :, QW:], A["w_kv_b"][0].rearrange("(k p) n -> p k n", p=P)).then_inc(w_loaded, 16)
            for n, name in enumerate(("q_a_norm_w", "kv_a_norm_w")):
                sp.dma_start(lat_gain[:, n * LORA:(n + 1) * LORA],
                             A[name][0:1, :].to_broadcast([P, LORA])).then_inc(consts, 16)
            for n, name in enumerate(("q_norm_w", "k_norm_w")):
                sp.dma_start(nope_gain[:, n:n + 1], A[name][0, 0:NOPE].unsqueeze(1)).then_inc(consts, 16)
                sp.dma_start(rope_gain[:, n, :], A[name][0:1, NOPE:QK].to_broadcast([P, ROPE])).then_inc(consts, 16)

            def load(t, s, u):
                rows = bass.ds(t * P, P)
                sp.wait_ge(latn_ready[s], u)
                sp.wait_ge(k_turned[s], u)
                sp.wait_ge(q_rotated[s], u)
                sp.dma_start(lat[s][:, :], S["tok"][rows, 0:2 * LORA]).then_inc(loaded[s], 16)
                sp.dma_start(kpe[s][:, :], S["tok"][rows, 2 * LORA + DNW:2 * LORA + DNW + ROPE]).then_inc(loaded[s], 16)
                sp.dma_start(trig[s][:, :, :], A["rope"][rows, :, :]).then_inc(loaded[s], 16)

            def store(t, s, u):
                cols = bass.ds(t * P, P)
                sp.wait_ge(qx_ready[s], u + 1)
                sp.wait_ge(kx_ready[s], u + 1)
                for x, to in ((qx, S["qT"]), (kx, S["kT"])):
                    sp.dma_start(to[:, 0:NOPE, cols].rearrange("h d t -> d h t"), x[s][:, 0:4, :]).then_inc(stored[s], 16)
                    for odd in range(2):
                        rows = slice(odd * ROPE, odd * ROPE + ROPE)
                        heads = to.rearrange("(g o) d t -> o g d t", o=2)[odd]
                        sp.dma_start(heads[:, NOPE:QK, cols].rearrange("g d t -> d g t"),
                                     x[s][rows, 4:6, :]).then_inc(stored[s], 16)
                sp.dma_start(S["v"][:, :, bass.ds(t, 1), :].rearrange("h p j d -> p (h j) d"), kv[s][:, :, NOPE:]).then_inc(v_stored[s], 16)

            tiles(sp, TILES, load, None, store)
            for s in range(2):
                sp.wait_ge(stored[s], 96 * ((TILES + 1 - s) // 2))
                sp.wait_ge(v_stored[s], 16 * ((TILES + 1 - s) // 2))

        @block.gpsimd
        def _(pool):
            make_identity(pool, ident, id_made)
            pool.wait_ge(consts, 97)
            per = 10

            def rotate(t, s, u):
                n = [0]

                def step(ins):
                    n[0] += 1
                    ins.then_inc(pool_step, 1)

                cos, sin = trig[s][:, 0, :], trig[s][:, 1, :]
                cos4, sin4 = (x.unsqueeze(1).to_broadcast([P, HEADS, HALF]) for x in (cos, sin))
                pool.wait_ge(loaded[s], 48 * (u + 1))
                step(pool.tensor_tensor(kg[:, :], kpe[s][:, :], rope_gain[:, 1, :], ALU.mult))
                pool.wait_ge(scaled[s], u + 1)
                step(pool.tensor_tensor(qg[:, :, :], qn[s][:, :, NOPE:],
                                        rope_gain[:, 0:1, :].to_broadcast([P, HEADS, ROPE]), ALU.mult))
                pool.wait_ge(pool_step, per * t + n[0])
                for m, (part, table) in enumerate(((0, cos), (1, sin), (0, sin), (1, cos))):
                    step(pool.tensor_tensor(kprod[:, m, :], kg[:, part * HALF:(part + 1) * HALF], table, ALU.mult))
                for m, (part, table) in enumerate(((0, cos4), (1, sin4), (0, sin4), (1, cos4))):
                    step(pool.tensor_tensor(qprod[:, m, :, :], qg[:, :, part * HALF:(part + 1) * HALF], table, ALU.mult))
                pool.wait_ge(pool_step, per * t + n[0])
                pool.wait_ge(k_rotated[s], u)
                pool.tensor_tensor(kturn[:, 0:HALF], kprod[:, 0, :], kprod[:, 1, :], ALU.subtract)
                pool.tensor_tensor(kturn[:, HALF:], kprod[:, 2, :], kprod[:, 3, :], ALU.add).then_inc(k_turned[s], 1)
                pool.wait_ge(turned[s], u)
                pool.tensor_tensor(qrope[s][:, :, 0:HALF], qprod[:, 0, :, :], qprod[:, 1, :, :], ALU.subtract)
                pool.tensor_tensor(qrope[s][:, :, HALF:], qprod[:, 2, :, :], qprod[:, 3, :, :],
                                   ALU.add).then_inc(q_rotated[s], 1)
                pool.wait_ge(k_turned[s], u + 1)
                pool.tensor_tensor(krope[s][:, :, :], kturn[:, :].unsqueeze(1).to_broadcast([P, HEADS, ROPE]),
                                   hs[s][:, 2, 4:8].unsqueeze(2).to_broadcast([P, HEADS, ROPE]),
                                   ALU.mult).then_inc(k_rotated[s], 1)

            tiles(pool, TILES, None, rotate)

        @block.scalar
        def _(act):
            act.wait_ge(w_loaded, 32)
            act.activation(w_hi[:, :, :], w_raw[:, :, :], ACT.Copy).then_inc(w_half, 1)
            act.wait_ge(consts, 97)

            def latents(t, s, u):
                act.wait_ge(loaded[s], 48 * (u + 1))
                act.wait_ge(lat_inv[s], u)
                for n in range(2):
                    act.activation(junk_l[:, n * LORA:(n + 1) * LORA], lat[s][:, n * LORA:(n + 1) * LORA], ACT.Square,
                                   accum_out=st[s][:, n:n + 1])
                act.wait_ge(sums_all[s], u)
                act.activation(junk_l[:, 2 * LORA:], kpe[s][:, :], ACT.Square, accum_out=st[s][:, 6:7]).then_inc(lat_sum[s], 1)
                act.wait_ge(lat_sum[s], u + 1)
                act.activation(st[s][:, 2:4], st[s][:, 0:2], ACT.Sqrt, bias=eps[:, :],
                               scale=1.0 / LORA).then_inc(lat_root[s], 1)
                act.wait_ge(lat_turned[s], u + 1)
                act.wait_ge(multiplied[s], u)
                act.activation(l_hi[s][:, :, :], pL[:, :, :], ACT.Copy).then_inc(l_hi_ready[s], 1)

            def heads(t, s, u):
                act.wait_ge(multiplied[s], u + 1)
                act.wait_ge(scaled[s], u)
                act.wait_ge(v_stored[s], 16 * u)
                act.activation(q[s][:, :, :].rearrange("p h d -> p (h d)"), pQ[:, 0:QW], ACT.Copy).then_inc(q_out[s], 1)
                act.activation(kv[s][:, :, :].rearrange("p h d -> p (h d)"), pKV[:, :], ACT.Copy).then_inc(kv_out[s], 1)
                act.wait_ge(kv_out[s], u + 1)
                act.wait_ge(q_out[s], u + 1)
                act.wait_ge(sums[1 - s], u + s)
                act.activation(junk[:, :], q[s][:, :, :].rearrange("p h d -> p (h d)"), ACT.Square)
                act.activation(junk_k[:, :, :], kv[s][:, :, 0:NOPE], ACT.Square).then_inc(squares[s], 1)
                act.wait_ge(sums_all[s], u + 1)
                act.activation(hs[s][:, 1, :], hs[s][:, 0, :], ACT.Sqrt, bias=eps[:, :],
                               scale=1.0 / QK).then_inc(roots[s], 1)

            def out(t, s, u):
                act.wait_ge(turned[s], u + 1)
                act.wait_ge(stored[s], 96 * u)
                act.activation(qx[s][:, 0:4, :], pX[:, 0, :, :], ACT.Copy, scale=nope_gain[:, 0:1])
                act.activation(qx[s][:, 4:6, :], pX[:, 2, 0:2, :], ACT.Copy).then_inc(qx_ready[s], 1)

            tiles(act, TILES, latents, heads, out)

        @block.vector
        def _(dve):
            dve.memset(eps[:, :], EPS).then_inc(consts, 1)
            dve.wait_ge(w_half, 1)
            dve.tensor_tensor(w_lo[:, :, :], w_raw[:, :, :], f(w_hi[:, :, :]), ALU.subtract).then_inc(w_ready, 1)
            dve.wait_ge(consts, 97)

            def latents(t, s, u):
                dve.wait_ge(lat_root[s], u + 1)
                dve.reciprocal(st[s][:, 4:6], st[s][:, 2:4]).then_inc(lat_inv[s], 1)
                dve.wait_ge(lat_inv[s], u + 1)
                dve.wait_ge(lat_turned[s], u)
                for n in range(2):
                    part = slice(n * LORA, (n + 1) * LORA)
                    m = dve.scalar_tensor_tensor(out=latn[s][:, part], in0=lat[s][:, part], scalar=st[s][:, 4 + n:5 + n],
                                                 in1=lat_gain[:, part], op0=ALU.mult, op1=ALU.mult)
                m.then_inc(latn_ready[s], 1)
                dve.wait_ge(l_hi_ready[s], u + 1)
                dve.tensor_tensor(l_lo[s][:, :, :], pL[:, :, :], f(l_hi[s][:, :, :]), ALU.subtract).then_inc(l_ready[s], 1)

            def heads(t, s, u):
                dve.wait_ge(squares[s], u + 1)
                dve.wait_ge(k_rotated[s], u)
                dve.tensor_reduce(hs[s][:, 0, 0:4], junk[:, :].rearrange("p (h d) -> p h d", h=HEADS), AX.X, ALU.add)
                dve.tensor_reduce(hs[s][:, 0, 4:8], junk_k[:, :, :], AX.X, ALU.add).then_inc(sums[s], 1)
                dve.wait_ge(sums[s], u + 1)
                dve.tensor_scalar(hs[s][:, 0, 4:8], hs[s][:, 0, 4:8], st[s][:, 6:7], None, ALU.add).then_inc(sums_all[s], 1)
                dve.wait_ge(roots[s], u + 1)
                dve.reciprocal(hs[s][:, 2, :], hs[s][:, 1, :]).then_inc(inverses[s], 1)
                dve.wait_ge(inverses[s], u + 1)
                dve.wait_ge(turned[s], u)
                dve.tensor_tensor(kn[s][:, :, :], kv[s][:, :, 0:NOPE],
                                  hs[s][:, 2, 4:8].unsqueeze(2).to_broadcast([P, HEADS, NOPE]), ALU.mult)
                dve.tensor_tensor(qn[s][:, :, :], q[s][:, :, :],
                                  hs[s][:, 2, 0:4].unsqueeze(2).to_broadcast([P, HEADS, QK]),
                                  ALU.mult).then_inc(scaled[s], 1)

            def out(t, s, u):
                dve.wait_ge(qx_ready[s], u + 1)
                dve.wait_ge(stored[s], 96 * u)
                dve.tensor_scalar(kx[s][:, 0:4, :], pX[:, 1, :, :], nope_gain[:, 1:2], None, ALU.mult)
                dve.tensor_copy(kx[s][:, 4:6, :], pX[:, 2, 2:4, :]).then_inc(kx_ready[s], 1)

            tiles(dve, TILES, latents, heads, out)

        @block.tensor
        def _(pe):
            pe.wait_ge(id_made, 2)

            def latents(t, s, u):
                pe.wait_ge(latn_ready[s], u + 1)
                pe.wait_ge(l_ready[1 - s], u + s)
                for k in range(4):
                    m = pe.transpose(pL[:, k, :], latn[s][:, k * P:k * P + P], ident[:, :])
                m.then_inc(lat_turned[s], 1)

            def heads(t, s, u):
                if isinstance(t, int) and t == 0:
                    pe.wait_ge(w_ready, 1)
                pe.wait_ge(l_ready[s], u + 1)
                pe.wait_ge(kv_out[1 - s], u + s)
                for to, w0, n, k0 in ((pQ[:, 0:512], 0, 512, 0), (pQ[:, 512:QW], 512, QW - 512, 0),
                                      (pKV[:, 0:512], QW, 512, 2), (pKV[:, 512:1024], QW + 512, 512, 2)):
                    for k in range(2):
                        for n_pass, (a, b) in enumerate(((l_hi, w_hi), (l_hi, w_lo), (l_lo, w_hi))):
                            m = pe.matmul(to, a[s][:, k0 + k, :], b[:, k, w0:w0 + n],
                                          start=(k == 0 and n_pass == 0), stop=(k == 1 and n_pass == 2))
                m.then_inc(multiplied[s], 1)

            def out(t, s, u):
                pe.wait_ge(q_rotated[s], u + 1)
                pe.wait_ge(k_rotated[s], u + 1)
                pe.wait_ge(kx_ready[1 - s], u + s)
                for h in range(HEADS):
                    pe.transpose(pX[:, 0, h, :], qn[s][:, h, 0:NOPE], ident[:, :])
                    pe.transpose(pX[:, 1, h, :], kn[s][:, h, :], ident[:, :])
                for g in range(2):
                    pe.transpose(pX[:, 2, g, :], qrope[s][:, 2 * g:2 * g + 2, :].rearrange("p h d -> p (h d)"), ident[:, :])
                    m = pe.transpose(pX[:, 2, 2 + g, :], krope[s][:, 2 * g:2 * g + 2, :].rearrange("p h d -> p (h d)"),
                                     ident[:, :])
                m.then_inc(turned[s], 1)

            tiles(pe, TILES, latents, heads, out)


def stage_conv(nc, A, S):
    with ExitStack() as ctx:
        r = Room(nc, ctx, "cv")
        MT, TAPS = 3 * DNW // P, 4
        NG, CG = 2, 3
        N = L // (NG * CG)
        YW = DN_PAD + L
        FULL = YW // P
        REST = YW - FULL * P
        u_hi = r.sb("u_hi", [P, KD, L], F32R)
        u_lo = r.sb("u_lo", [P, KD, L], F32R)
        w_raw = [r.sb(f"w_raw{i}", [P, KD, P]) for i in range(2)]
        w_hi = [r.sb(f"w_hi{i}", [P, KD, P], F32R) for i in range(2)]
        w_lo = [r.sb(f"w_lo{i}", [P, KD, P], F32R) for i in range(2)]
        ident = r.sb("ident", [P, P])
        taps_in = r.sb("taps_in", [TAPS * MT, P])
        taps = r.sb("taps", [P, TAPS * MT])
        raw = r.sb("raw", [P, TAPS - 1 + L])
        y = [r.sb(f"y{i}", [P, YW]) for i in range(2)]
        ob = r.sb("ob", [P, FULL + 1, P])
        pG = [r.ps(f"pG{i}", [P, CG, 512]) for i in range(NG)]
        pT = [r.ps(f"pT{i}", [P, 4, P]) for i in range(2)]

        consts, id_made, taps_turned, zeroed = r.sem("consts"), r.sem("id_made"), r.sem("taps_turned"), r.sem("zeroed")
        taps_ready, u_loaded = r.sem("taps_ready"), r.sem("u_loaded")
        w_loaded, w_half, w_ready = r.sems("w_loaded"), r.sems("w_half"), r.sems("w_ready")
        product, raw_out, conv_step = r.sems("product"), r.sems("raw_out", NG), r.sem("conv_step")
        convolved, active, turned = r.sems("convolved"), r.sems("active"), r.sems("turned")
        out_act, out_dve, stored = r.sem("out_act"), r.sem("out_dve"), r.sem("stored")
        QUADS = [(q, list(b)) for q, b in enumerate(np.array_split(np.arange(FULL + 1), -(-(FULL + 1) // 4)))]
        ACT_QUADS, DVE_QUADS = (len(QUADS) + 1) // 2, len(QUADS) // 2

        block = ctx.enter_context(nc.Block())

        @block.sync
        def _(sp):
            sp.dma_start(taps_in[:, :], A["dn_conv_w"][0].rearrange("j (m p) -> (j m) p", p=P)).then_inc(consts, 16)

            def load(t, s, u):
                sp.wait_ge(w_ready[s], u)
                sp.wait_ge(consts, 16)
                sp.dma_start(w_raw[s][:, :, :], A["w_in"][0].rearrange("(k p) n -> p k n", p=P)[
                    :, :, bass.ds(C_QKV + t * P, P)]).then_inc(w_loaded[s], 16)
                if isinstance(t, int) and t == 0:
                    for k in range(KD):
                        sp.dma_start(f(u_hi[:, k, :]), S["uT"][0, :, k, 0:L]).then_inc(u_loaded, 16)
                        sp.dma_start(f(u_lo[:, k, :]), S["uT"][1, :, k, 0:L]).then_inc(u_loaded, 16)

            def store(t, s, u):
                cols = bass.ds(t * P, P)
                sp.wait_ge(out_act, ACT_QUADS * (t + 1))
                sp.dma_start(S["dtok"][0:FULL * P, cols].rearrange("(j p) d -> p j d", p=P),
                             ob[:, 0:FULL, :]).then_inc(stored, 16)
                sp.dma_start(S["dtok"][FULL * P:YW, cols], ob[0:REST, FULL, :]).then_inc(stored, 16)

            tiles(sp, MT, load, None, store)
            sp.wait_ge(stored, 32 * MT)

        @block.gpsimd
        def _(pool):
            make_identity(pool, ident, id_made)
            pool.memset(raw[:, 0:TAPS - 1], 0.0).then_inc(zeroed, 1)
            for s in range(2):
                pool.memset(y[s][:, 0:DN_PAD], 0.0).then_inc(zeroed, 1)

        @block.scalar
        def _(act):
            def split(t, s, u):
                act.wait_ge(w_loaded[s], 16 * (u + 1))
                act.wait_ge(product[s], NG * u)
                act.activation(w_hi[s][:, :, :], w_raw[s][:, :, :], ACT.Copy).then_inc(w_half[s], 1)

            def out(t, s, u):
                for g in range(NG):
                    act.wait_ge(product[s], NG * u + g + 1)
                    act.wait_ge(convolved[1 - s], u + s)
                    o = TAPS - 1 + g * CG * N
                    act.activation(raw[:, o:o + CG * N].rearrange("p (c n) -> p c n", c=CG),
                                   pG[g][:, :, 0:N], ACT.Copy).then_inc(raw_out[g], 1)

            def silu(t, s, u):
                act.wait_ge(convolved[s], u + 1)
                act.activation(y[s][:, DN_PAD:], y[s][:, DN_PAD:], ACT.Silu).then_inc(active[s], 1)
                act.wait_ge(stored, 32 * t)
                for q, blocks in QUADS[0::2]:
                    act.wait_ge(turned[s], len(QUADS) * u + q + 1)
                    if q == len(QUADS) - 1:
                        act.wait_ge(out_dve, DVE_QUADS * (t + 1))
                    act.activation(ob[:, int(blocks[0]):int(blocks[-1]) + 1, :], pT[q % 2][:, 0:len(blocks), :],
                                   ACT.Copy).then_inc(out_act, 1)

            tiles(act, MT, split, out, silu)

        @block.vector
        def _(dve):
            dve.wait_ge(taps_turned, 1)
            dve.tensor_copy(taps[:, :], pT[0][:, 0, 0:TAPS * MT]).then_inc(taps_ready, 1)
            dve.wait_ge(taps_ready, 1)
            dve.wait_ge(zeroed, 3)

            def split(t, s, u):
                dve.wait_ge(w_half[s], u + 1)
                dve.tensor_tensor(w_lo[s][:, :, :], w_raw[s][:, :, :], f(w_hi[s][:, :, :]), ALU.subtract).then_inc(w_ready[s], 1)

            def convolve(t, s, u):
                for g in range(NG):
                    dve.wait_ge(raw_out[g], t + 1)
                dve.wait_ge(turned[s], len(QUADS) * u)
                acc = y[s][:, DN_PAD:]
                for j in range(TAPS):
                    tap = taps[:, bass.ds(j * MT + t, 1)]
                    if j == 0:
                        dve.tensor_scalar(acc, raw[:, 0:L], tap, None, ALU.mult).then_inc(conv_step, 1)
                    else:
                        dve.wait_ge(conv_step, (TAPS - 1) * t + j)
                        m = dve.scalar_tensor_tensor(out=acc, in0=raw[:, j:j + L], scalar=tap, in1=acc,
                                                     op0=ALU.mult, op1=ALU.add)
                        m.then_inc(conv_step if j < TAPS - 1 else convolved[s], 1)

            def out(t, s, u):
                dve.wait_ge(stored, 32 * t)
                for q, blocks in QUADS[1::2]:
                    dve.wait_ge(turned[s], len(QUADS) * u + q + 1)
                    dve.tensor_copy(ob[:, int(blocks[0]):int(blocks[-1]) + 1, :], pT[q % 2][:, 0:len(blocks), :]).then_inc(out_dve, 1)

            tiles(dve, MT, split, convolve, out)

        @block.tensor
        def _(pe):
            pe.wait_ge(id_made, 2)
            pe.wait_ge(consts, 16)
            pe.transpose(pT[0][:, 0, 0:TAPS * MT], taps_in[:, :], ident[0:TAPS * MT, 0:TAPS * MT]).then_inc(taps_turned, 1)

            def multiply(t, s, u):
                if isinstance(t, int) and t == 0:
                    pe.wait_ge(u_loaded, 32 * KD)
                pe.wait_ge(w_ready[s], u + 1)
                for g in range(NG):
                    pe.wait_ge(raw_out[g], t)
                    for k in range(KD):
                        for n_pass, (a, b) in enumerate(((w_hi, u_hi), (w_hi, u_lo), (w_lo, u_hi))):
                            for c in range(CG):
                                o = (g * CG + c) * N
                                m = pe.matmul(pG[g][:, c, 0:N], a[s][:, k, :], b[:, k, o:o + N],
                                              start=(k == 0 and n_pass == 0), stop=(k == KD - 1 and n_pass == 2))
                    m.then_inc(product[s], 1)

            def turn(t, s, u):
                pe.wait_ge(active[s], u + 1)
                if isinstance(t, int) and t == 0:
                    pe.wait_ge(taps_ready, 1)
                for q, blocks in QUADS:
                    if q % 2 == 0:
                        pe.wait_ge(out_act, ACT_QUADS * t + q // 2)
                    else:
                        pe.wait_ge(out_dve, DVE_QUADS * t + q // 2)
                    for n, j in enumerate(map(int, blocks)):
                        w = P if j < FULL else REST
                        m = pe.transpose(pT[q % 2][0:w, n, :], y[s][:, j * P:j * P + w], ident[:, :])
                    m.then_inc(turned[s], 1)

            tiles(pe, MT, None, multiply, turn)


BIG = 1e30
LEVELS = 6
DT = -(-CHUNKS // 2)
UNITS = 4
NC = 2 * DT
GC, NGC, EG, ED, BG, BETA, NBETA = range(7)
U_, WT_, QT_, QK_, KD_ = range(5)
C2 = P // 2
HALVES = (slice(0, C2), slice(C2, P))


def turns(eng, n, prep, level, final):
    def at(t):
        return (t, t % 2, t // 2)

    def step(t, nxt):
        for lv in range(1, LEVELS):
            level(lv, *t)
            if nxt is not None:
                prep(lv - 1, *nxt)
        final(*t)

    for i in range(LEVELS - 1):
        prep(i, *at(0))
    pairs = (n - 1) // 2
    with eng.Fori(0, pairs) as p:
        step((2 * p, 0, p), (2 * p + 1, 1, p))
        step((2 * p + 1, 1, p), (2 * p + 2, 0, p + 1))
    for t in range(2 * pairs, n):
        step(at(t), at(t + 1) if t + 1 < n else None)


def stage_gates(nc, A, S):
    with ExitStack() as ctx:
        r = Room(nc, ctx, "gt")
        W = NC * 2
        ident = r.sb("ident", [P, P])
        tri = r.sb("tri", [P, P])
        same = r.sb("same", [P, P])
        only = [r.sb(f"only{i}", [P, P]) for i in range(2)]
        ones = r.sb("ones", [P, 1])
        zeros = r.sb("zeros", [CHUNK, 3 * DNW])
        ab = r.sb("ab", [P, NC, 2 * HEADS])
        bias = r.sb("bias", [P, HEADS])
        a_log = r.sb("a_log", [P, HEADS])
        a_exp = r.sb("a_exp", [P, HEADS])
        xa = r.sb("xa", [P, NC, HEADS])
        xabs = r.sb("xabs", [P, NC, HEADS])
        e1 = r.sb("e1", [P, NC, HEADS])
        l1 = r.sb("l1", [P, NC, HEADS])
        sp_ = r.sb("softplus", [P, NC, HEADS])
        g4 = r.sb("g4", [P, NC, HEADS])
        eb = r.sb("eb", [P, NC, HEADS])
        eb1 = r.sb("eb1", [P, NC, HEADS])
        beta4 = r.sb("beta4", [P, NC, HEADS])
        g = r.sb("g", [P, NC, 2])
        gl = r.sb("gl", [P, NC, 2])
        gd = r.sb("gd", [P, NC, 2])
        egl = r.sb("egl", [P, NC, 2, 2])
        sc = r.sb("sc", [P, 7, NC, 2])
        gct = r.sb("gct", [W, P])
        pA = r.ps("pA", [P, 512])
        pB = r.ps("pB", [P, 512])
        pC = r.ps("pC", [P, 512])
        pool_step, cleared, masks, loaded = r.sem("pool_step"), r.sem("cleared"), r.sem("masks"), r.sem("loaded")
        chain_v, chain_a = r.sem("chain_v"), r.sem("chain_a")
        sums, turned, stored = r.sem("sums"), r.sem("turned"), r.sem("stored")
        block = ctx.enter_context(nc.Block())

        @block.sync
        def _(sp):
            assert DN_PAD + N_META == CHUNK
            sp.wait_ge(cleared, 1)
            rows = S["tok"][:, TOKW - 2 * HEADS:TOKW]
            for hh in range(2):
                sp.dma_start(ab[hh * C2:hh * C2 + C2, 1:CHUNKS, :],
                             rows[N_META:L, :].rearrange("(c i) e -> i c e", i=CHUNK)).then_inc(loaded, 16)
                sp.dma_start(ab[hh * C2 + DN_PAD:hh * C2 + C2, 0, :], rows[0:N_META, :]).then_inc(loaded, 16)
            sp.dma_start(bias[:, :], A["dn_dt_bias"][0:1, :].to_broadcast([P, HEADS])).then_inc(loaded, 16)
            sp.dma_start(a_log[:, :], A["dn_A_log"][0:1, :].to_broadcast([P, HEADS])).then_inc(loaded, 16)
            sp.dma_start(S["dtok"][DN_PAD + L:, :], zeros[:, :]).then_inc(stored, 16)
            sp.wait_ge(chain_a, 7)
            sp.wait_ge(chain_v, 12)
            sp.dma_start(S["gcr"], gct[:, :]).then_inc(stored, 16)
            sp.dma_start(S["egl"], egl[:, :, :, :]).then_inc(stored, 16)
            sp.dma_start(S["sc"], sc[:, :, :, :]).then_inc(stored, 16)
            sp.wait_ge(stored, 64)

        @block.gpsimd
        def _(pool):
            n = [0]

            def step(ins):
                n[0] += 1
                ins.then_inc(pool_step, 1)

            def keep(ap, pattern, base, mult, fill=0.0, op=ALU.is_ge):
                pool.wait_ge(pool_step, n[0])
                step(pool.affine_select(out=ap, in_=ap, compare_op=op, fill=fill, base=base, pattern=pattern,
                                        channel_multiplier=mult))

            step(pool.memset(ab[:, :, :], 0.0))
            step(pool.memset(zeros[:, :], 0.0))
            pool.wait_ge(pool_step, 2)
            pool.memset(ones[:, :], 1.0).then_inc(cleared, 1)
            for m in (tri, same, *only):
                step(pool.memset(m[:, :], 1.0))
            keep(only[0][:, :], [[0, P]], C2 - 1, -1)
            keep(only[1][:, :], [[0, P]], -C2, 1)
            keep(tri[:, :], [[1, P]], 0, -1)
            for m in (tri, same):
                keep(m[:, :], [[-C2, 2], [0, C2]], 0, 1)
            keep(same[:, :], [[C2, 2], [0, C2]], C2 - 1, -1)
            step(pool.memset(ident[:, :], 0.0))
            keep(ident[:, :], [[-1, P]], 0, 1, 1.0, ALU.not_equal)
            pool.wait_ge(pool_step, n[0])
            pool.memset(g[:, :, :], 0.0).then_inc(masks, 1)

        @block.scalar
        def _(act):
            act.preload_act_table_set("natural_log_exp_and_others")
            act.wait_ge(chain_v, 1)
            act.activation(xabs[:, :, :], xa[:, :, :], ACT.Abs).then_inc(chain_a, 1)
            act.wait_ge(chain_a, 1)
            act.activation(e1[:, :, :], xabs[:, :, :], ACT.Exp, scale=-1.0).then_inc(chain_a, 1)
            act.wait_ge(chain_a, 2)
            act.wait_ge(cleared, 1)
            act.activation(l1[:, :, :], e1[:, :, :], ACT.Ln, bias=ones[:, :])
            act.activation(eb[:, :, :], ab[:, :, HEADS:], ACT.Exp, scale=-1.0)
            act.activation(a_exp[:, :], a_log[:, :], ACT.Exp).then_inc(chain_a, 1)
            act.wait_ge(sums, 1)
            flat = sc[:, :, :, :].rearrange("p k c g -> p k (c g)")
            act.activation(flat[:, GC, :], pA[:, 0:W], ACT.Copy).then_inc(chain_a, 1)
            act.activation(flat[:, NGC, :], pA[:, 0:W], ACT.Copy, scale=-1.0)
            act.activation(flat[:, EG, :], pA[:, 0:W], ACT.Exp)
            act.activation(gl[:, :, :].rearrange("p c g -> p (c g)"), pA[:, W:2 * W], ACT.Copy)
            for hh in range(2):
                o = act.activation(egl[:, :, :, hh].rearrange("p c g -> p (c g)"), pB[:, hh * W:(hh + 1) * W], ACT.Exp)
            o.then_inc(chain_a, 1)
            act.wait_ge(chain_v, 9)
            act.activation(flat[:, ED, :], gd[:, :, :].rearrange("p c g -> p (c g)"), ACT.Exp).then_inc(chain_a, 1)
            act.wait_ge(turned, 1)
            act.activation(gct[:, :], pC[0:W, 0:P], ACT.Copy).then_inc(chain_a, 1)

        @block.vector
        def _(dve):
            n = [0]

            def step(ins, wait=True):
                n[0] += 1
                ins.then_inc(chain_v, 1)
                if wait:
                    dve.wait_ge(chain_v, n[0])

            dve.wait_ge(loaded, 96)
            step(dve.tensor_tensor(xa[:, :, :], ab[:, :, 0:HEADS],
                                   bias[:, :].unsqueeze(1).to_broadcast([P, NC, HEADS]), ALU.add))
            dve.wait_ge(chain_a, 3)
            step(dve.scalar_tensor_tensor(out=sp_[:, :, :], in0=xa[:, :, :], scalar=0.0, in1=l1[:, :, :],
                                          op0=ALU.max, op1=ALU.add))
            step(dve.tensor_tensor(g4[:, :, :], sp_[:, :, :], a_exp[:, :].unsqueeze(1).to_broadcast([P, NC, HEADS]), ALU.mult))
            step(dve.tensor_scalar(eb1[:, :, :], eb[:, :, :], 1.0, None, ALU.add))
            step(dve.reciprocal(beta4[:, :, :], eb1[:, :, :]))
            dve.wait_ge(masks, 1)
            for hh in range(2):
                rows = HALVES[hh]
                dve.tensor_scalar(g[rows, 0:CHUNKS, :], g4[rows, 0:CHUNKS, hh::2], -1.0, None, ALU.mult)
                o = dve.tensor_copy(sc[rows, BETA, :, :], beta4[rows, :, hh::2])
            step(o)
            for hh in range(2):
                o = dve.memset(g[hh * C2:hh * C2 + 32, 0, :], 0.0)
            step(o)
            for hh in range(2):
                o = dve.memset(g[hh * C2 + 32:hh * C2 + DN_PAD, 0, :], 0.0)
            step(o)
            dve.wait_ge(chain_a, 5)
            step(dve.tensor_tensor(gd[:, :, :], gl[:, :, :], sc[:, GC, :, :], ALU.subtract))
            step(dve.tensor_tensor(sc[:, BG, :, :], sc[:, BETA, :, :], sc[:, EG, :, :], ALU.mult))
            step(dve.tensor_scalar(sc[:, NBETA, :, :], sc[:, BETA, :, :], -1.0, None, ALU.mult))
            dve.wait_ge(chain_a, 6)
            step(dve.tensor_copy(g4[:, 0, 0:1], sc[:, ED, 0, 0:1]))

        @block.tensor
        def _(pe):
            pe.wait_ge(chain_v, 8)
            gf = g[:, :, :].rearrange("p c g -> p (c g)")
            pe.matmul(pA[:, 0:W], tri[:, :], gf, start=True, stop=True)
            pe.matmul(pA[:, W:2 * W], same[:, :], gf, start=True, stop=True)
            pe.matmul(pB[:, 0:W], only[0][:, :], gf, start=True, stop=True)
            pe.matmul(pB[:, W:2 * W], only[1][:, :], gf, start=True, stop=True).then_inc(sums, 1)
            pe.wait_ge(chain_a, 4)
            pe.transpose(pC[0:W, 0:P], sc[:, GC, :, :].rearrange("p c g -> p (c g)"), ident[:, :]).then_inc(turned, 1)


def stage_intra(nc, A, S):
    with ExitStack() as ctx:
        r = Room(nc, ctx, "dn")
        ident = r.sb("ident", [P, P])
        level_of = [r.sb(f"level{i}", [P, P]) for i in range(LEVELS + 1)]
        strict_off = r.sb("strict_off", [P, P])
        causal_off = r.sb("causal_off", [P, P])
        eps = r.sb("eps", [P, 1])
        sc = r.sb("sc", [P, 7, NC, 2])
        qkv = [r.sb(f"qkv{i}", [P, 2, 6, P]) for i in range(2)]
        grow = [r.sb(f"grow{i}", [P, UNITS, P]) for i in range(2)]
        scs = [r.sb(f"scs{i}", [P, 7, UNITS]) for i in range(2)]
        sq = r.sb("sq", [P, 2, 4, P])
        nrm = [r.sb(f"nrm{i}", [P, 3, 2, 4]) for i in range(2)]
        offs = r.sb("offs", [P, 2, UNITS, P])
        dec = r.sb("dec", [P, 2, UNITS, P])
        egr = r.sb("egr", [P, UNITS, P])
        tin = r.sb("tin", [P, UNITS, 2, P])
        kbg = [r.sb(f"kbg{i}", [P, UNITS, P]) for i in range(2)]
        vb = [r.sb(f"vb{i}", [P, UNITS, P]) for i in range(2)]
        kq = r.sb("kq", [P, UNITS, 2, P])
        nn = r.sb("nn", [P, UNITS, 2, P])
        xx = [r.sb(f"xx{i}", [P, UNITS, 2, P]) for i in range(2)]
        nt = [r.sb(f"nt{i}", [P, LEVELS - 1, UNITS, P]) for i in range(2)]
        pr = r.sb("pr", [P, UNITS, P])
        out = [r.sb(f"out{i}", [P, UNITS, 5, P]) for i in range(2)]
        pT = [r.ps(f"pT{i}", [P, 2, 2, P]) for i in range(2)]
        pK = [r.ps(f"pK{i}", [P, 2, 2, P]) for i in range(2)]
        pP = [r.ps(f"pP{i}", [P, 2, 2, P]) for i in range(2)]
        pQ = [r.ps(f"pQ{i}", [P, 2, 2, P]) for i in range(2)]

        consts, pool_step, masks = r.sem("consts"), r.sem("pool_step"), r.sem("masks")
        x_part = r.sem("x_part")
        loaded, squared, summed, logs, inv = (r.sems(x) for x in ("loaded", "squared", "summed", "logs", "inv"))
        scs_ready, offs_ready, decayed, scaled = (r.sems(x) for x in ("scs_ready", "offs_ready", "decayed", "scaled"))
        kd_ready, turned, kq_ready, qg_ready = (r.sems(x) for x in ("kd_ready", "turned", "kq_ready", "qg_ready"))
        kk, n_ready, nq_ready, n_turned, nt_out = (r.sems(x) for x in ("kk", "n_ready", "nq_ready", "n_turned", "nt_out"))
        x_ready, final_mm, w_out, u_out, all_out, stored = (
            r.sems(x) for x in ("x_ready", "final_mm", "w_out", "u_out", "all_out", "stored"))
        p_done, p_out, q_done, x_step = (r.sems(x) for x in ("p_done", "p_out", "q_done", "x_step"))
        STEPS = LEVELS - 1

        block = ctx.enter_context(nc.Block())

        def nothing(*a):
            pass

        @block.sync
        def _(sp):
            sp.dma_start(sc[:, :, :, :], S["sc"]).then_inc(consts, 16)

            def prep(i, t, s, u):
                if i != 0:
                    return
                sp.wait_ge(qg_ready[s], u)
                rows = S["dtok"][bass.ds(t * P, P), :].rearrange("(c t) (e h d) -> h t c e d", c=2, h=2, d=P)
                for hh in range(2):
                    for c in range(2):
                        sp.dma_start(qkv[s][HALVES[hh], c, :, :], rows[hh, :, c]).then_inc(loaded[s], 16)
                sp.dma_start(grow[s][:, :, :].rearrange("p u n -> p (u n)"),
                             S["gcr"][bass.ds(t * UNITS, UNITS), :].rearrange("u n -> (u n)")
                             .unsqueeze(0).to_broadcast([P, UNITS * P])).then_inc(loaded[s], 16)

            def final(t, s, u):
                sp.wait_ge(qg_ready[s], u + 1)
                sp.wait_ge(kd_ready[s], u + 1)
                sp.wait_ge(nq_ready[s], u + 1)
                sp.wait_ge(all_out[s], u + 1)
                sp.wait_ge(consts, 16)
                sp.dma_start(S["prod"][bass.ds(2 * t, 2)].rearrange("c p g k n -> p c (g k n)"),
                             out[s][:, :, :, :].rearrange("p (c g) k n -> p c (g k n)", c=2)).then_inc(stored[s], 16)

            turns(sp, DT, prep, nothing, final)
            for s in range(2):
                sp.wait_ge(stored[s], 16 * ((DT + 1 - s) // 2))

        @block.gpsimd
        def _(pool):
            n = [0]

            def step(ins):
                n[0] += 1
                ins.then_inc(pool_step, 1)

            def settle():
                pool.wait_ge(pool_step, n[0])

            def keep(ap, pattern, base, mult, op, fill):
                settle()
                step(pool.affine_select(out=ap, in_=ap, compare_op=op, fill=fill, base=base, pattern=pattern,
                                        channel_multiplier=mult))

            step(pool.memset(eps[:, :], EPS))
            step(pool.memset(strict_off[:, :], 0.0))
            step(pool.memset(causal_off[:, :], 0.0))
            for b in level_of:
                step(pool.memset(b[:, :], 1.0))
            for i, b in enumerate(level_of):
                w = 2 ** i
                keep(b[:, :], [[-w, P // w], [0, w]], 0, 1, ALU.is_ge, 0.0)
                keep(b[:, :], [[w, P // w], [0, w]], w - 1, -1, ALU.is_ge, 0.0)
            keep(strict_off[:, :], [[-1, P]], 0, 1, ALU.is_gt, BIG)
            keep(strict_off[:, :], [[C2, 2], [0, C2]], C2 - 1, -1, ALU.is_ge, BIG)
            keep(causal_off[:, :], [[1, P]], 0, -1, ALU.is_ge, -BIG)
            keep(causal_off[:, :], [[-C2, 2], [0, C2]], 0, 1, ALU.is_ge, -BIG)
            settle()
            step(pool.tensor_copy(ident[:, :], level_of[0][:, :]))
            for lv in range(LEVELS):
                settle()
                o = pool.tensor_tensor(level_of[lv][:, :], level_of[lv + 1][:, :], level_of[lv][:, :], ALU.subtract)
                if lv < LEVELS - 1:
                    step(o)
            o.then_inc(masks, 1)
            pool.wait_ge(masks, 1)
            pool.wait_ge(consts, 16)

            def prep(i, t, s, u):
                if i == 0:
                    pool.wait_ge(loaded[s], 80 * (u + 1))
                    pool.wait_ge(nq_ready[s], u)
                    pool.tensor_copy(scs[s][:, :, :], sc[:, :, bass.ds(2 * t, 2), :].rearrange("p k c g -> p k (c g)")
                                     ).then_inc(scs_ready[s], 1)
                    pool.wait_ge(decayed[1 - s], u + s)
                    for m, off in enumerate((strict_off, causal_off)):
                        o = pool.tensor_tensor(offs[:, m, :, :], grow[s][:, :, :],
                                               off[:, :].unsqueeze(1).to_broadcast([P, UNITS, P]), ALU.add)
                    o.then_inc(offs_ready[s], 1)
                if i == 2:
                    pool.wait_ge(scaled[s], u + 1)
                    pool.wait_ge(scs_ready[s], u + 1)
                    pool.wait_ge(final_mm[s], 2 * u)
                    pool.wait_ge(stored[s], 16 * u)
                    def per_row(k):
                        return scs[s][:, k, :].unsqueeze(2).to_broadcast([P, UNITS, P])

                    pool.tensor_tensor(kbg[s][:, :, :], tin[:, :, 0, :], per_row(BG), ALU.mult)
                    for c in range(2):
                        pool.tensor_tensor(vb[s][:, 2 * c:2 * c + 2, :], qkv[s][:, c, 4:6, :],
                                           scs[s][:, BETA, 2 * c:2 * c + 2].unsqueeze(2).to_broadcast([P, 2, P]), ALU.mult)
                    o = pool.tensor_tensor(out[s][:, :, KD_, :], tin[:, :, 0, :], per_row(ED), ALU.mult)
                    o.then_inc(kd_ready[s], 1)
                if i == 3:
                    pool.wait_ge(kq_ready[s], 2 * u + 2)
                    pool.wait_ge(decayed[s], u + 1)
                    pool.tensor_tensor(out[s][:, :, QT_, :], kq[:, :, 1, :], egr[:, :, :], ALU.mult).then_inc(qg_ready[s], 1)
                if i == 4:
                    pool.wait_ge(nt_out[s], u + 1)
                    pool.wait_ge(n_ready[s], 2 * u + 2)
                    nn4 = nn[:, :, :, :].rearrange("p u a n -> p (u a) n")
                    xx4 = xx[s][:, :, :, :].rearrange("p u a n -> p (u a) n")
                    pool.tensor_tensor(xx4, nn4, level_of[0][:, :].unsqueeze(1).to_broadcast([P, 2 * UNITS, P]),
                                       ALU.mult).then_inc(x_part, 1)
                    for lv in range(1, LEVELS):
                        pool.tensor_tensor(nt[s][:, lv - 1, :, :], nn[:, :, 1, :],
                                           level_of[lv][:, :].unsqueeze(1).to_broadcast([P, UNITS, P]), ALU.mult)
                    pool.wait_ge(x_part, t + 1)
                    pool.tensor_tensor(xx4, xx4, ident[:, :].unsqueeze(1).to_broadcast([P, 2 * UNITS, P]),
                                       ALU.add).then_inc(x_ready[s], 1)

            turns(pool, DT, prep, nothing, nothing)

        @block.scalar
        def _(act):
            act.preload_act_table_set("natural_log_exp_and_others")
            act.wait_ge(masks, 1)

            def prep(i, t, s, u):
                if i == 0:
                    act.wait_ge(loaded[s], 80 * (u + 1))
                    act.wait_ge(summed[1 - s], u + s)
                    act.activation(sq[:, :, :, :], qkv[s][:, :, 0:4, :], ACT.Square).then_inc(squared[s], 1)
                    act.wait_ge(summed[s], u + 1)
                    act.activation(nrm[s][:, 1], nrm[s][:, 0], ACT.Ln, bias=eps[:, :]).then_inc(logs[s], 1)
                    act.wait_ge(logs[s], u + 1)
                    act.activation(nrm[s][:, 2], nrm[s][:, 1], ACT.Exp, scale=-0.5).then_inc(inv[s], 1)
                if i == 1:
                    act.wait_ge(offs_ready[s], u + 1)
                    act.wait_ge(nq_ready[1 - s], u + s)
                    act.wait_ge(qg_ready[1 - s], u + s)
                    for un in range(UNITS):
                        act.activation(dec[:, 0, un, :], offs[:, 0, un, :], ACT.Exp, bias=scs[s][:, GC, un:un + 1], scale=-1.0)
                        act.activation(dec[:, 1, un, :], offs[:, 1, un, :], ACT.Exp, bias=scs[s][:, NGC, un:un + 1])
                    act.activation(egr[:, :, :], grow[s][:, :, :], ACT.Exp).then_inc(decayed[s], 1)
                if i == 2:
                    act.wait_ge(kk[1 - s], 2 * (u + s))
                    for c in range(2):
                        act.wait_ge(turned[s], 2 * u + c + 1)
                        act.activation(kq[:, 2 * c:2 * c + 2, :, :], pT[c][:, :, :, :], ACT.Copy).then_inc(kq_ready[s], 1)
                if i == 4:
                    act.wait_ge(x_ready[1 - s], u + s)
                    for c in range(2):
                        act.wait_ge(n_turned[s], 2 * u + c + 1)
                        o = act.activation(nn[:, 2 * c:2 * c + 2, 1, :], pT[c][:, :, 0, :], ACT.Copy)
                    o.then_inc(nt_out[s], 1)

            def level(lv, t, s, u):
                for c in range(2):
                    act.wait_ge(p_done[c], STEPS * t + lv)
                    act.activation(pr[:, 2 * c:2 * c + 2, :], pP[c][:, 0, :, :], ACT.Copy).then_inc(p_out[c], 1)

            def final(t, s, u):
                for c in range(2):
                    act.wait_ge(final_mm[s], 2 * u + c + 1)
                    act.activation(out[s][:, 2 * c:2 * c + 2, WT_, :], pP[c][:, 0, :, :], ACT.Copy).then_inc(w_out[s], 1)

            turns(act, DT, prep, level, final)

        @block.vector
        def _(dve):
            dve.wait_ge(masks, 1)

            def prep(i, t, s, u):
                if i == 0:
                    dve.wait_ge(squared[s], u + 1)
                    dve.tensor_reduce(nrm[s][:, 0], sq[:, :, :, :], AX.X, ALU.add).then_inc(summed[s], 1)
                if i == 1:
                    dve.wait_ge(inv[s], u + 1)
                    dve.wait_ge(kd_ready[1 - s], u + s)
                    dve.wait_ge(turned[1 - s], 2 * (u + s))
                    for un in range(UNITS):
                        c, gg = un // 2, un % 2
                        dve.tensor_scalar(tin[:, un, 0, :], qkv[s][:, c, 2 + gg, :], nrm[s][:, 2, c, 2 + gg:3 + gg], None, ALU.mult)
                        o = dve.tensor_scalar(tin[:, un, 1, :], qkv[s][:, c, gg, :], nrm[s][:, 2, c, gg:gg + 1],
                                              float(P) ** -0.5, ALU.mult, ALU.mult)
                    o.then_inc(scaled[s], 1)
                if i == 4:
                    dve.wait_ge(decayed[s], u + 1)
                    dve.wait_ge(x_ready[1 - s], u + s)
                    dve.wait_ge(stored[s], 16 * u)
                    for c in range(2):
                        dve.wait_ge(kk[s], 2 * u + c + 1)
                        for gg in range(2):
                            un = 2 * c + gg
                            o = dve.scalar_tensor_tensor(out=nn[:, un, 0, :], in0=pK[c][:, gg, 0, :], scalar=scs[s][:, NBETA, un:un + 1],
                                                         in1=dec[:, 0, un, :], op0=ALU.mult, op1=ALU.mult)
                        o.then_inc(n_ready[s], 1)
                    for c in range(2):
                        o = dve.tensor_tensor(out[s][:, 2 * c:2 * c + 2, QK_, :], pK[c][:, :, 1, :],
                                              dec[:, 1, 2 * c:2 * c + 2, :], ALU.mult)
                    o.then_inc(nq_ready[s], 1)

            def level(lv, t, s, u):
                for c in range(2):
                    dve.wait_ge(q_done[c], STEPS * t + lv)
                    if lv == 1:
                        dve.wait_ge(x_ready[s], u + 1)
                    x, q = xx[s][:, 2 * c:2 * c + 2, :, :], pQ[c][:, :, :, :]
                    if lv == STEPS:
                        x, q = x[:, :, 1, :], q[:, :, 1, :]
                    dve.tensor_tensor(x, q, x, ALU.add).then_inc(x_step[c], 1)

            def final(t, s, u):
                for c in range(2):
                    dve.wait_ge(w_out[s], 2 * u + c + 1)
                    o = dve.tensor_copy(out[s][:, 2 * c:2 * c + 2, U_, :], pP[c][:, 1, :, :])
                    o.then_inc(u_out[s] if c == 0 else all_out[s], 1)

            turns(dve, DT, prep, level, final)

        @block.tensor
        def _(pe):
            pe.wait_ge(masks, 1)

            def prep(i, t, s, u):
                if i == 2:
                    pe.wait_ge(scaled[s], u + 1)
                    pe.wait_ge(nt_out[1 - s], u + s)
                    for c in range(2):
                        for gg in range(2):
                            for a in range(2):
                                m = pe.transpose(pT[c][:, gg, a, :], tin[:, 2 * c + gg, a, :], ident[:, :])
                        m.then_inc(turned[s], 1)
                if i == 3:
                    pe.wait_ge(nq_ready[1 - s], u + s)
                    for c in range(2):
                        pe.wait_ge(kq_ready[s], 2 * u + c + 1)
                        for gg in range(2):
                            m = pe.matmul(pK[c][:, gg, :, :].rearrange("p a n -> p (a n)"), kq[:, 2 * c + gg, 0, :],
                                          kq[:, 2 * c + gg, :, :].rearrange("p a n -> p (a n)"), start=True, stop=True)
                        m.then_inc(kk[s], 1)
                if i == 4:
                    for c in range(2):
                        pe.wait_ge(n_ready[s], 2 * u + c + 1)
                        for gg in range(2):
                            m = pe.transpose(pT[c][:, gg, 0, :], nn[:, 2 * c + gg, 0, :], ident[:, :])
                        m.then_inc(n_turned[s], 1)

            def level(lv, t, s, u):
                if lv == 1:
                    pe.wait_ge(x_ready[s], u + 1)
                    pe.wait_ge(u_out[1 - s], u + s)
                    pe.wait_ge(all_out[1 - s], u + s)
                for c in range(2):
                    pe.wait_ge(x_step[c], STEPS * t + lv - 1)
                    for gg in range(2):
                        un = 2 * c + gg
                        m = pe.matmul(pP[c][:, 0, gg, :], nt[s][:, lv - 1, un, :], xx[s][:, un, 0, :], start=True, stop=True)
                    m.then_inc(p_done[c], 1)
                for c in range(2):
                    pe.wait_ge(p_out[c], STEPS * t + lv)
                    for gg in range(2):
                        un = 2 * c + gg
                        if lv < STEPS:
                            pe.matmul(pQ[c][:, gg, 0, :], xx[s][:, un, 1, :], pr[:, un, :], start=True, stop=True)
                        m = pe.matmul(pQ[c][:, gg, 1, :], pr[:, un, :], xx[s][:, un, 1, :], start=True, stop=True)
                    m.then_inc(q_done[c], 1)

            def final(t, s, u):
                pe.wait_ge(kd_ready[s], u + 1)
                for c in range(2):
                    pe.wait_ge(x_step[c], STEPS * (t + 1))
                    for gg in range(2):
                        un = 2 * c + gg
                        pe.matmul(pP[c][:, 0, gg, :], kbg[s][:, un, :], xx[s][:, un, 1, :], start=True, stop=True)
                        m = pe.matmul(pP[c][:, 1, gg, :], xx[s][:, un, 1, :], vb[s][:, un, :], start=True, stop=True)
                    m.then_inc(final_mm[s], 1)

            turns(pe, DT, prep, level, final)


def stage_scan(nc, A, S):
    with ExitStack() as ctx:
        r = Room(nc, ctx, "sn")
        egl = r.sb("egl", [P, NC, 2, 2])
        prod = [r.sb(f"prod{i}", [P, 2, 5, P]) for i in range(2)]
        st = [r.sb(f"st{i}", [P, HEADS, P]) for i in range(2)]
        vn = r.sb("vn", [P, 2, P])
        osb = [r.sb(f"osb{i}", [P, 2, P]) for i in range(2)]
        pW = r.ps("pW", [P, 2, P])
        pS = [r.ps(f"pS{i}", [P, 2, P]) for i in range(2)]
        pO = [[r.ps(f"pO{i}{j}", [P, P]) for j in range(2)] for i in range(2)]
        consts, cleared = r.sem("consts"), r.sem("cleared")
        loaded, ws, v_ready, ks, s_ready, o_done, o_out, stored = (
            r.sems(x) for x in ("loaded", "ws", "v_ready", "ks", "s_ready", "o_done", "o_out", "stored"))
        block = ctx.enter_context(nc.Block())

        @block.sync
        def _(sp):
            sp.dma_start(egl[:, :, :, :], S["egl"]).then_inc(consts, 16)

            def load(t, s, u):
                sp.wait_ge(o_done[s], u)
                sp.wait_ge(consts, 16)
                sp.dma_start(prod[s][:, :, :, :], S["prod"][bass.ds(t, 1)].rearrange("a p g k n -> (a p) g k n")
                             ).then_inc(loaded[s], 16)

            def store(t, s, u):
                sp.wait_ge(o_out[s], u + 1)
                sp.wait_ge(consts, 16)
                rows = S["o_dn"][bass.ds(t * CHUNK, CHUNK), :].rearrange("t (g h d) -> h t g d", h=2, d=P)
                for hh in range(2):
                    sp.dma_start(rows[hh], osb[s][HALVES[hh], :, :]).then_inc(stored[s], 16)

            tiles(sp, CHUNKS, load, None, store)
            for s in range(2):
                sp.wait_ge(stored[s], 32 * ((CHUNKS + 1 - s) // 2))

        @block.scalar
        def _(act):
            def out(t, s, u):
                act.wait_ge(o_done[s], u + 1)
                act.wait_ge(stored[s], 32 * u)
                for gg in range(2):
                    o = act.activation(osb[s][:, gg, :], pO[s][gg][:, :], ACT.Copy)
                o.then_inc(o_out[s], 1)

            tiles(act, CHUNKS, None, out)

        @block.vector
        def _(dve):
            dve.memset(st[0][:, :, :], 0.0).then_inc(cleared, 1)
            dve.wait_ge(cleared, 1)
            dve.wait_ge(consts, 16)

            def scan(t, s, u):
                dve.wait_ge(ws[s], u + 1)
                dve.wait_ge(o_done[1 - s], u + s)
                dve.tensor_tensor(vn[:, :, :], prod[s][:, :, U_, :], pW[:, :, :], ALU.subtract).then_inc(v_ready[s], 1)
                dve.wait_ge(ks[s], u + 1)
                for h in range(HEADS):
                    o = dve.scalar_tensor_tensor(
                        out=st[1 - s][:, h, :], in0=st[s][:, h, :],
                        scalar=egl[:, bass.ds(t, 1), h // 2, h % 2], in1=pS[h % 2][:, h // 2, :],
                        op0=ALU.mult, op1=ALU.add)
                o.then_inc(s_ready[1 - s], 1)

            tiles(dve, CHUNKS, None, scan)

        @block.tensor
        def _(pe):
            pe.wait_ge(cleared, 1)

            def scan(t, s, u):
                pe.wait_ge(loaded[s], 16 * (u + 1))
                pe.wait_ge(s_ready[s], u if s == 0 else u + 1)
                for h in range(HEADS):
                    gg, rows = h // 2, HALVES[h % 2]
                    m = pe.matmul(pW[rows, gg, :], prod[s][:, gg, WT_, rows], st[s][:, h, :], start=True, stop=True)
                m.then_inc(ws[s], 1)
                pe.wait_ge(o_out[s], u)
                for h in range(HEADS):
                    gg, rows = h // 2, HALVES[h % 2]
                    pe.matmul(pO[s][gg][rows, :], prod[s][:, gg, QT_, rows], st[s][:, h, :], start=True, stop=False,
                              skip_group_check=True)
                pe.wait_ge(v_ready[s], u + 1)
                for h in range(HEADS):
                    gg, rows = h // 2, HALVES[h % 2]
                    m = pe.matmul(pS[h % 2][:, gg, :], prod[s][rows, gg, KD_, :], vn[rows, gg, :], start=True, stop=True)
                m.then_inc(ks[s], 1)
                for gg in range(2):
                    m = pe.matmul(pO[s][gg][:, :], prod[s][:, gg, QK_, :], vn[:, gg, :], start=False, stop=True,
                                  skip_group_check=True)
                m.then_inc(o_done[s], 1)

            tiles(pe, CHUNKS, None, scan)


def stage_attention(nc, A, S):
    with ExitStack() as ctx:
        r = Room(nc, ctx, "at")
        BLOCKS = [(h, i) for h in range(2) for i in range(TILES)]
        NB = len(BLOCKS)
        CH = [-(-(i + 1) // 4) for _, i in BLOCKS]
        BEFORE = [sum(CH[:b]) for b in range(NB + 1)]
        CT = BEFORE[NB]
        QG = -(-TILES // 4)
        GT = 2 * QG
        FIRST = [(gi // QG) * TILES + 4 * (gi % QG) for gi in range(GT)]
        TURNS = HEADS // 2
        NPS = 3
        assert CT % NPS == 0 and CT % 2 == 0 and NB % 2 == 0 and GT % 2 == 0
        SCALE = float(QK) ** -0.5
        k_raw = r.sb("k_raw", [P, LP])
        kr_raw = r.sb("kr_raw", [P, LP])
        v_raw = r.sb("v_raw", [P, TILES, VD])
        k_hi = [r.sb(f"k_hi{i}", [P, LP], F32R) for i in range(2)]
        k_lo = [r.sb(f"k_lo{i}", [P, LP], F32R) for i in range(2)]
        kr = [r.sb(f"kr{i}", [P, LP], F32R) for i in range(2)]
        v = [r.sb(f"v{i}", [P, TILES, 2, VD], F32R) for i in range(2)]
        q_raw = [r.sb(f"q_raw{i}", [P, 4 * P]) for i in range(2)]
        qr_raw = [r.sb(f"qr_raw{i}", [P, 4 * P]) for i in range(2)]
        q_hi = [r.sb(f"q_hi{i}", [P, 4 * P], F32R) for i in range(2)]
        q_lo = [r.sb(f"q_lo{i}", [P, 4 * P], F32R) for i in range(2)]
        qr_hi = [r.sb(f"qr_hi{i}", [P, 4 * P], F32R) for i in range(2)]
        qr_lo = [r.sb(f"qr_lo{i}", [ROPE, 4 * P], F32R) for i in range(2)]
        s_row = [r.sb(f"s_row{i}", [P, LP]) for i in range(2)]
        p_row = [r.sb(f"p_row{i}", [P, LP]) for i in range(2)]
        pt_hi = [r.sb(f"pt_hi{i}", [P, 4, P], F32R) for i in range(2)]
        pt_lo = [r.sb(f"pt_lo{i}", [P, 4, P], F32R) for i in range(2)]
        stat = [r.sb(f"stat{i}", [P, 12]) for i in range(2)]
        o_lo = [r.sb(f"o_lo{i}", [P, VD]) for i in range(2)]
        o_sb = [r.sb(f"o_sb{i}", [P, VD]) for i in range(2)]
        ident = r.sb("ident", [P, P])
        mask = r.sb("mask", [P, P])
        pS = [r.ps(f"pS{i}", [P, 512]) for i in range(NPS)]
        pT = [r.ps(f"pT{i}", [P, 4, P]) for i in range(2)]
        pO = [r.ps(f"pO{i}", [P, 512]) for i in range(2)]

        id_made, mask_made = r.sem("id_made"), r.sem("mask_made")
        k_loaded, kr_loaded, v_loaded, kv_half, kv_split = (r.sem(x) for x in ("k_loaded", "kr_loaded", "v_loaded", "kv_half", "kv_split"))
        q_loaded, q_half, q_ready = r.sems("q_loaded"), r.sem("q_half"), r.sem("q_ready")
        qk_done, s_out, maxed, max_step, p_ready = (r.sem(x) for x in ("qk_done", "s_out", "maxed", "max_step", "p_ready"))
        t_done, hi_done, lo_done, pv_done = (r.sem(x) for x in ("t_done", "hi_done", "lo_done", "pv_done"))
        inv_done, o2_done, o_done, stored = r.sem("inv_done"), r.sem("o2_done"), r.sem("o_done"), r.sems("stored")
        PIECE_AT = {3: (1, 0), 6: (1, 1), 9: (1, 2), TILES + 3: (0, 0), TILES + 6: (0, 1), TILES + 9: (0, 2)}
        GROUP_AT = {FIRST[gi] - 2: gi for gi in range(1, GT)}

        block = ctx.enter_context(nc.Block())

        @block.sync
        def _(sp):
            def load_kv(head, n):
                sp.wait_ge(kv_split, 3 * n)
                sp.wait_ge(id_made, 2)
                one = bass.ds(head, 1)
                sp.dma_start(k_raw[:, :], S["kT"][one, 0:NOPE, :].rearrange("h d t -> (h d) t")).then_inc(k_loaded, 16)
                for half in HALVES:
                    sp.dma_start(kr_raw[half, :], S["kT"][one, NOPE:QK, :].rearrange("h d t -> (h d) t")).then_inc(kr_loaded, 16)
                sp.dma_start(v_raw[:, :, :], S["v"][one, :, :, :].rearrange("h p j d -> (h p) j d")).then_inc(v_loaded, 16)

            def load_q(p, gi):
                n = min(4, TILES - 4 * (gi % QG)) * P
                cols = slice(4 * P * (gi % QG), 4 * P * (gi % QG) + n)
                s = gi % 2
                sp.wait_ge(q_ready, GT * p + max(gi - 1, 0))
                sp.wait_ge(id_made, 2)
                q = S["qT"][bass.ds(2 * p + gi // QG, 1), :, cols]
                sp.dma_start(q_raw[s][:, 0:n], q[:, 0:NOPE, :].rearrange("h d t -> (h d) t")).then_inc(q_loaded[s], 16)
                for half in HALVES:
                    sp.dma_start(qr_raw[s][half, 0:n], q[:, NOPE:QK, :].rearrange("h d t -> (h d) t")).then_inc(q_loaded[s], 16)

            load_kv(0, 0)
            with sp.Fori(0, TURNS) as p:
                load_q(p, 0)
                load_q(p, 1)
                load_kv(2 * p + 1, 2 * p + 1)
                for gi in range(2, QG + 1):
                    load_q(p, gi)
                load_kv((2 * p + 2) % HEADS, 2 * p + 2)
                for gi in range(QG + 1, GT):
                    load_q(p, gi)

        @block.gpsimd
        def _(pool):
            make_identity(pool, ident, id_made)
            pool.memset(mask[:, :], 0.0).then_inc(mask_made, 1)
            pool.wait_ge(mask_made, 1)
            pool.affine_select(out=mask[:, :], in_=mask[:, :], compare_op=ALU.is_ge, fill=-BIG, base=0,
                               pattern=[[-1, P]], channel_multiplier=1).then_inc(mask_made, 1)
            with pool.Fori(0, TURNS) as p:
                for b, (h, i) in enumerate(BLOCKS):
                    pool.wait_ge(o_done, NB * p + b + 1)
                    pool.dma_start(S["o_mla"][i * P:i * P + P, bass.ds((2 * p + h) * VD, VD)],
                                   o_sb[b % 2][:, :]).then_inc(stored[b % 2], 16)
            for s in range(2):
                pool.wait_ge(stored[s], 16 * TURNS * NB // 2)

        @block.scalar
        def _(act):
            act.wait_ge(id_made, 2)

            def piece(n, slot, j, free):
                if j == 0:
                    act.wait_ge(k_loaded, 16 * (n + 1))
                    act.wait_ge(pv_done, free)
                    act.activation(k_hi[slot][:, :], k_raw[:, :], ACT.Copy).then_inc(kv_half, 1)
                elif j == 1:
                    act.wait_ge(kr_loaded, 32 * (n + 1))
                    act.activation(kr[slot][:, :], kr_raw[:, :], ACT.Copy).then_inc(kv_half, 1)
                else:
                    act.wait_ge(v_loaded, 16 * (n + 1))
                    act.activation(v[slot][:, :, 0, :], v_raw[:, :, :], ACT.Copy).then_inc(kv_half, 1)

            def group(p, gi):
                s, n = gi % 2, min(4, TILES - 4 * (gi % QG)) * P
                act.wait_ge(q_loaded[s], 48 * (QG * p + gi // 2 + 1))
                act.wait_ge(qk_done, CT * p + (BEFORE[FIRST[gi - 1]] if gi >= 2 else 0))
                act.activation(q_hi[s][:, 0:n], q_raw[s][:, 0:n], ACT.Copy)
                act.activation(qr_hi[s][:, 0:n], qr_raw[s][:, 0:n], ACT.Copy).then_inc(q_half, 1)

            def exp(p, b):
                i = BLOCKS[b][1]
                act.wait_ge(maxed, NB * p + b + 1)
                act.wait_ge(t_done, CT * p + BEFORE[max(b - 1, 0)])
                act.wait_ge(inv_done, NB * p + max(b - 1, 0))
                act.activation(p_row[b % 2][:, 0:(i + 1) * P], s_row[b % 2][:, 0:(i + 1) * P], ACT.Exp,
                               bias=stat[b % 2][:, 8:9], accum_out=stat[b % 2][:, 9:10]).then_inc(p_ready, 1)

            def hi(p, b):
                for g in range(CH[b]):
                    m = BEFORE[b] + g
                    n = min(4, BLOCKS[b][1] + 1 - 4 * g)
                    act.wait_ge(t_done, CT * p + m + 1)
                    act.wait_ge(pv_done, CT * p + max(m - 1, 0))
                    act.activation(pt_hi[m % 2][:, 0:n, :], pT[m % 2][:, 0:n, :], ACT.Copy).then_inc(hi_done, 1)

            def o2(p, b):
                act.wait_ge(pv_done, CT * p + BEFORE[b + 1])
                act.wait_ge(inv_done, NB * p + b + 1)
                act.wait_ge(o_done, NB * p + max(b - 1, 0))
                act.activation(o_lo[b % 2][:, :], pO[b % 2][:, VD:2 * VD], ACT.Copy,
                               scale=stat[b % 2][:, 10:11]).then_inc(o2_done, 1)

            for j in range(3):
                piece(0, 0, j, 0)
            with act.Fori(0, TURNS) as p:
                group(p, 0)
                exp(p, 0)
                for b in range(NB):
                    if b in PIECE_AT:
                        slot, j = PIECE_AT[b]
                        piece(2 * p + 2 - slot, slot, j, CT * p + (0 if slot else BEFORE[TILES]))
                    if b in GROUP_AT:
                        group(p, GROUP_AT[b])
                    hi(p, b)
                    o2(p, b)
                    if b + 1 < NB:
                        exp(p, b + 1)

        @block.vector
        def _(dve):
            dve.wait_ge(mask_made, 2)

            def piece(n, slot, j):
                dve.wait_ge(kv_half, 3 * n + j + 1)
                if j == 0:
                    o = dve.tensor_tensor(k_lo[slot][:, :], k_raw[:, :], f(k_hi[slot][:, :]), ALU.subtract)
                elif j == 1:
                    low = HALVES[1]
                    o = dve.tensor_tensor(kr[slot][low, :], kr_raw[low, :], f(kr[slot][low, :]), ALU.subtract)
                else:
                    o = dve.tensor_tensor(v[slot][:, :, 1, :], v_raw[:, :, :], f(v[slot][:, :, 0, :]), ALU.subtract)
                o.then_inc(kv_split, 1)

            def group(p, gi):
                s, n = gi % 2, min(4, TILES - 4 * (gi % QG)) * P
                dve.wait_ge(q_half, GT * p + gi + 1)
                dve.tensor_tensor(q_lo[s][:, 0:n], q_raw[s][:, 0:n], f(q_hi[s][:, 0:n]), ALU.subtract)
                dve.tensor_tensor(qr_lo[s][:, 0:n], qr_raw[s][0:ROPE, 0:n], f(qr_hi[s][0:ROPE, 0:n]),
                                  ALU.subtract).then_inc(q_ready, 1)

            def scores(p, b):
                i = BLOCKS[b][1]
                row, st = s_row[b % 2], stat[b % 2]
                dve.wait_ge(p_ready, NB * p + max(b - 1, 0))
                for c in range(CH[b]):
                    m = BEFORE[b] + c
                    n = min(4, i + 1 - 4 * c) * P
                    bank = pS[m % NPS]
                    dve.wait_ge(qk_done, CT * p + m + 1)
                    last = c == CH[b] - 1
                    whole = n - P if last else n
                    if whole:
                        o = dve.tensor_scalar(row[:, 4 * P * c:4 * P * c + whole], bank[:, 0:whole], SCALE, None,
                                              ALU.mult, ALU.max, accum_out=st[:, c:c + 1])
                    if last:
                        o = dve.scalar_tensor_tensor(out=row[:, i * P:i * P + P], in0=bank[:, whole:n], scalar=SCALE,
                                                     in1=mask[:, :], op0=ALU.mult, op1=ALU.add)
                    o.then_inc(s_out, 1)
                full = CH[b] if i % 4 else CH[b] - 1
                dve.wait_ge(s_out, CT * p + BEFORE[b + 1])
                dve.tensor_reduce(st[:, full:full + 1], row[:, i * P:i * P + P], AX.X, ALU.max).then_inc(max_step, 1)
                dve.wait_ge(max_step, NB * p + b + 1)
                dve.tensor_reduce(st[:, 8:9], st[:, 0:full + 1], AX.X, ALU.max, negate=True).then_inc(maxed, 1)

            def lo(p, b):
                for g in range(CH[b]):
                    m = BEFORE[b] + g
                    n = min(4, BLOCKS[b][1] + 1 - 4 * g)
                    dve.wait_ge(hi_done, CT * p + m + 1)
                    dve.tensor_tensor(pt_lo[m % 2][:, 0:n, :], pT[m % 2][:, 0:n, :], f(pt_hi[m % 2][:, 0:n, :]),
                                      ALU.subtract).then_inc(lo_done, 1)

            def norm(p, b):
                dve.reciprocal(stat[b % 2][:, 10:11], stat[b % 2][:, 9:10]).then_inc(inv_done, 1)
                dve.wait_ge(o2_done, NB * p + b + 1)
                dve.wait_ge(stored[b % 2], 16 * (NB // 2 * p + b // 2))
                dve.scalar_tensor_tensor(out=o_sb[b % 2][:, :], in0=pO[b % 2][:, 0:VD], scalar=stat[b % 2][:, 10:11],
                                         in1=o_lo[b % 2][:, :], op0=ALU.mult, op1=ALU.add).then_inc(o_done, 1)

            for j in range(3):
                piece(0, 0, j)
            with dve.Fori(0, TURNS) as p:
                group(p, 0)
                scores(p, 0)
                for b in range(NB):
                    if b in PIECE_AT:
                        slot, j = PIECE_AT[b]
                        piece(2 * p + 2 - slot, slot, j)
                    if b in GROUP_AT:
                        group(p, GROUP_AT[b])
                    if b + 1 < NB:
                        scores(p, b + 1)
                    lo(p, b)
                    norm(p, b)

        @block.tensor
        def _(pe):
            pe.wait_ge(id_made, 2)

            def scores(p, b):
                h, i = BLOCKS[b]
                gi = h * QG + i // 4
                s, o = gi % 2, (i % 4) * P
                if i % 4 == 0:
                    pe.wait_ge(q_ready, GT * p + gi + 1)
                if i == 0:
                    pe.wait_ge(kv_split, 6 * p + 3 * h + 3)
                for c in range(CH[b]):
                    m = BEFORE[b] + c
                    n = min(4, i + 1 - 4 * c) * P
                    keys = slice(4 * P * c, 4 * P * c + n)
                    pe.wait_ge(s_out, CT * p + max(m - NPS + 1, 0))
                    pairs = ((q_hi[s], k_hi[h]), (q_hi[s], k_lo[h]), (q_lo[s], k_hi[h]), (qr_hi[s], kr[h]))
                    for x, (a, w) in enumerate(pairs):
                        pe.matmul(pS[m % NPS][:, 0:n], a[:, o:o + P], w[:, keys], start=(x == 0), stop=False)
                    pe.matmul(pS[m % NPS][:, 0:n], qr_lo[s][:, o:o + P], kr[h][0:ROPE, keys], start=False,
                              stop=True).then_inc(qk_done, 1)

            def values(p, b):
                h, i = BLOCKS[b]

                def turn(g):
                    m = BEFORE[b] + g
                    pe.wait_ge(lo_done, CT * p + max(m - 1, 0))
                    for j in range(4 * g, min(4 * g + 4, i + 1)):
                        t = pe.transpose(pT[m % 2][:, j - 4 * g, :], p_row[b % 2][:, j * P:j * P + P], ident[:, :])
                    t.then_inc(t_done, 1)

                pe.wait_ge(p_ready, NB * p + b + 1)
                turn(0)
                for g in range(CH[b]):
                    m = BEFORE[b] + g
                    if g + 1 < CH[b]:
                        turn(g + 1)
                    pe.wait_ge(lo_done, CT * p + m + 1)
                    if g == 0:
                        pe.wait_ge(o_done, NB * p + max(b - 1, 0))
                    for j in range(4 * g, min(4 * g + 4, i + 1)):
                        n = j - 4 * g
                        pe.matmul(pO[b % 2][:, 0:2 * VD], pt_hi[m % 2][:, n, :], v[h][:, j, :, :].rearrange("p a d -> p (a d)"),
                                  start=(j == 0), stop=False)
                        t = pe.matmul(pO[b % 2][:, 0:VD], pt_lo[m % 2][:, n, :], v[h][:, j, 0, :],
                                      start=False, stop=(j == i))
                    t.then_inc(pv_done, 1)

            with pe.Fori(0, TURNS) as p:
                scores(p, 0)
                for b in range(NB):
                    if b + 1 < NB:
                        scores(p, b + 1)
                    values(p, b)


def four_tiles(eng, n, front, mid, tail, back):
    def at(t):
        return (t, t % 2, t // 2) if 0 <= t < n else None

    def step(*at_each):
        for part, tile in zip((front, mid, tail, back), at_each):
            if part and tile is not None:
                part(*tile)

    def single(t):
        step(at(t + 1), at(t), at(t - 2), at(t - 1))

    for t in range(-1, 2):
        single(t)
    turns = (n - 4) // 2
    with eng.Fori(0, turns) as p:
        t = [(2 * p + i, i % 2, p + i // 2) for i in range(5)]
        step(t[3], t[2], t[0], t[1])
        step(t[4], t[3], t[1], t[2])
    for t in range(2 * turns + 2, n + 2):
        single(t)


def stage_out(nc, A, S):
    with ExitStack() as ctx:
        r = Room(nc, ctx, "ot")
        NH = 2 * HEADS
        REST = L - (TILES - 1) * P
        w_hi = r.sb("w_hi", [P, KD, D], F32R)
        w_lo = r.sb("w_lo", [P, KD, D], F32R)
        w_raw = [r.sb(f"w_raw{i}", [P, D]) for i in range(2)]
        gain = r.sb("gain", [P, NH, P])
        ffn_gain = r.sb("ffn_gain", [P, D])
        ident = r.sb("ident", [P, P])
        eps = r.sb("eps", [P, 1])
        y = [r.sb(f"y{i}", [P, NH, P]) for i in range(2)]
        z = [r.sb(f"z{i}", [P, DNW]) for i in range(2)]
        ez = [r.sb(f"ez{i}", [P, DNW]) for i in range(2)]
        zg = r.sb("zg", [P, DNW])
        sq = [r.sb(f"sq{i}", [P, NH, P]) for i in range(2)]
        yg = [r.sb(f"yg{i}", [P, NH, P]) for i in range(2)]
        mix = [r.sb(f"mix{i}", [P, D]) for i in range(2)]
        m_hi = [r.sb(f"m_hi{i}", [P, KD, P], F32R) for i in range(2)]
        m_lo = [r.sb(f"m_lo{i}", [P, KD, P], F32R) for i in range(2)]
        st = [r.sb(f"st{i}", [P, 3, NH]) for i in range(2)]
        res = [r.sb(f"res{i}", [P, D]) for i in range(2)]
        h2 = [r.sb(f"h2{i}", [P, D]) for i in range(2)]
        st2 = [r.sb(f"st2{i}", [P, 3]) for i in range(2)]
        junk = r.sb("junk", [P, D])
        xn = [r.sb(f"xn{i}", [P, D]) for i in range(2)]
        u_hi = [r.sb(f"u_hi{i}", [P, KD, P], F32R) for i in range(2)]
        u_lo = [r.sb(f"u_lo{i}", [P, KD, P], F32R) for i in range(2)]
        pT = r.ps("pT", [P, KD, P])
        pU = r.ps("pU", [P, KD, P])
        pP = [r.ps(f"pP{i}", [P, 2, 512]) for i in range(2)]

        w_loaded, w_half, w_ready = r.sems("w_loaded"), r.sem("w_half"), r.sem("w_ready")
        consts, id_made, eps_set, head_loaded = r.sem("consts"), r.sem("id_made"), r.sem("eps_set"), r.sem("head_loaded")
        y_loaded, z_loaded, res_loaded = r.sems("y_loaded"), r.sems("z_loaded"), r.sems("res_loaded")
        squared, z_exp, summed, logs, rooted = (r.sems(x) for x in ("squared", "z_exp", "summed", "logs", "rooted"))
        z_one, z_inv, gated, yg_ready, mixed = r.sem("z_one"), r.sems("z_inv"), r.sem("gated"), r.sems("yg_ready"), r.sems("mixed")
        turned, m_half, m_ready = r.sems("turned"), r.sems("m_half"), r.sems("m_ready")
        multiplied, h2_ready, h2_sum, h2_log, h2_root = (
            r.sems(x) for x in ("multiplied", "h2_ready", "h2_sum", "h2_log", "h2_root"))
        xn_ready, xn_turned, u_half, u_ready = (r.sems(x) for x in ("xn_ready", "xn_turned", "u_half", "u_ready"))
        h2_stored, u_stored = r.sems("h2_stored"), r.sems("u_stored")

        block = ctx.enter_context(nc.Block())

        @block.sync
        def _(sp):
            for h in range(NH):
                sp.dma_start(gain[:, h, :], A["mla_out_norm_w" if h < HEADS else "dn_out_norm_w"][0:1, :].to_broadcast([P, P])
                             ).then_inc(consts, 16)
            sp.dma_start(ffn_gain[:, :], A["ffn_norm_w"][0:1, :].to_broadcast([P, D])).then_inc(consts, 16)

            def load(t, s, u):
                rows = slice(0, P)
                mla, dn = bass.ds(t * P, P), bass.ds(t * P + DN_PAD, P)
                if isinstance(t, int) and t == TILES - 1:
                    rows, mla, dn = slice(0, REST), slice(t * P, L), slice(t * P + DN_PAD, L + DN_PAD)
                sp.wait_ge(mixed[s], u)
                sp.wait_ge(id_made, 2)
                sp.dma_start(y[s][rows, 0:HEADS, :], S["o_mla"][mla, :].rearrange("t (h d) -> t h d", d=P)).then_inc(y_loaded[s], 16)
                sp.dma_start(y[s][rows, HEADS:, :], S["o_dn"][dn, :].rearrange("t (h d) -> t h d", d=P)).then_inc(y_loaded[s], 16)
                sp.dma_start(z[s][rows, :], S["tok"][mla, 2 * LORA:2 * LORA + DNW]).then_inc(z_loaded[s], 16)
                if isinstance(t, int) and t == 0:
                    for k in range(KD):
                        if k >= 2:
                            sp.wait_ge(w_ready, k - 1)
                        sp.dma_start(w_raw[k % 2][:, :], A["w_out"][0, k * P:k * P + P, :]).then_inc(w_loaded[k % 2], 16)

            four_tiles(sp, TILES, load, None, None, None)

        @block.gpsimd
        def _(pool):
            make_identity(pool, ident, id_made)
            pool.dma_start(res[0][0:N_META, :], A["meta_tokens"]).then_inc(head_loaded, 16)
            pool.dma_start(res[0][N_META:P, :], A["x"][0, 0:P - N_META, :]).then_inc(res_loaded[0], 16)
            pool.dma_start(res[1][:, :], A["x"][0, P - N_META:2 * P - N_META, :]).then_inc(res_loaded[1], 16)
            pool.wait_ge(consts, 16 * (NH + 1))

            def gate(t, s, u):
                pool.wait_ge(z_inv[s], u + 1)
                pool.wait_ge(yg_ready[1 - s], u + s)
                pool.tensor_tensor(zg[:, :], z[s][:, :], ez[s][:, :], ALU.mult).then_inc(gated, 1)
                pool.wait_ge(mixed[s], u)
                pool.wait_ge(gated, 2 * t + 1)
                pool.tensor_tensor(yg[s][:, HEADS:, :].rearrange("p h d -> p (h d)"),
                                   y[s][:, HEADS:, :].rearrange("p h d -> p (h d)"), zg[:, :], ALU.mult).then_inc(gated, 1)
                pool.tensor_tensor(yg[s][:, 0:HEADS, :], y[s][:, 0:HEADS, :], gain[:, 0:HEADS, :], ALU.mult)
                pool.wait_ge(gated, 2 * t + 2)
                pool.tensor_tensor(yg[s][:, HEADS:, :], yg[s][:, HEADS:, :], gain[:, HEADS:, :],
                                   ALU.mult).then_inc(yg_ready[s], 1)

            def residual(t, s, u):
                if isinstance(t, int) and t + 2 >= TILES:
                    return
                pool.wait_ge(h2_ready[s], u + 1)
                if isinstance(t, int) and t + 2 == TILES - 1:
                    pool.dma_start(res[s][0:REST, :], A["x"][0, SEQ - REST:SEQ, :]).then_inc(res_loaded[s], 16)
                else:
                    pool.dma_start(res[s][:, :], A["x"][0, bass.ds((t + 2) * P - N_META, P), :]).then_inc(res_loaded[s], 16)

            def store(t, s, u):
                cols = bass.ds(t * P, P)
                pool.wait_ge(u_ready[s], u + 1)
                pool.dma_start(S["u2T"][0, :, :, cols], f(u_hi[s][:, :, :])).then_inc(u_stored[s], 16)
                pool.dma_start(S["u2T"][1, :, :, cols], f(u_lo[s][:, :, :])).then_inc(u_stored[s], 16)

            four_tiles(pool, TILES, gate, None, store, residual)
            for s in range(2):
                pool.wait_ge(u_stored[s], 32 * ((TILES + 1 - s) // 2))

        @block.scalar
        def _(act):
            act.preload_act_table_set("natural_log_exp_and_others")
            act.wait_ge(eps_set, 1)
            for k in range(KD):
                act.wait_ge(w_loaded[k % 2], 16 * (k // 2 + 1))
                act.activation(w_hi[:, k, :], w_raw[k % 2][:, :], ACT.Copy).then_inc(w_half, 1)

            def norm(t, s, u):
                act.wait_ge(y_loaded[s], 32 * (u + 1))
                act.wait_ge(summed[s], u)
                act.activation(sq[s][:, :, :], y[s][:, :, :], ACT.Square).then_inc(squared[s], 1)
                act.wait_ge(z_loaded[s], 16 * (u + 1))
                act.wait_ge(yg_ready[s], u)
                act.activation(ez[s][:, :], z[s][:, :], ACT.Exp, scale=-1.0).then_inc(z_exp[s], 1)
                act.wait_ge(summed[s], u + 1)
                act.activation(st[s][:, 1, :], st[s][:, 0, :], ACT.Ln, bias=eps[:, :], scale=1.0 / P).then_inc(logs[s], 1)
                act.wait_ge(mixed[s], u)
                act.wait_ge(logs[s], u + 1)
                act.activation(st[s][:, 2, :], st[s][:, 1, :], ACT.Exp, scale=-0.5).then_inc(rooted[s], 1)

            def hi(t, s, u):
                act.wait_ge(turned[s], u + 1)
                act.wait_ge(multiplied[s], u)
                act.activation(m_hi[s][:, :, :], pT[:, :, :], ACT.Copy).then_inc(m_half[s], 1)

            def u_part(t, s, u):
                act.wait_ge(xn_turned[s], u + 1)
                act.wait_ge(u_stored[s], 32 * u)
                act.activation(u_hi[s][:, :, :], pU[:, :, :], ACT.Copy).then_inc(u_half[s], 1)

            def norm2(t, s, u):
                act.wait_ge(h2_ready[s], u + 1)
                act.dma_start(S["h2"][bass.ds(t * P, P), :], h2[s][:, :]).then_inc(h2_stored[s], 16)
                act.activation(junk[:, :], h2[s][:, :], ACT.Square, accum_out=st2[s][:, 0:1]).then_inc(h2_sum[s], 1)
                act.wait_ge(h2_sum[s], u + 1)
                act.activation(st2[s][:, 1:2], st2[s][:, 0:1], ACT.Ln, bias=eps[:, :], scale=1.0 / D).then_inc(h2_log[s], 1)
                act.wait_ge(h2_log[s], u + 1)
                act.activation(st2[s][:, 2:3], st2[s][:, 1:2], ACT.Exp, scale=-0.5).then_inc(h2_root[s], 1)

            four_tiles(act, TILES, norm, hi, u_part, norm2)
            for s in range(2):
                act.wait_ge(h2_stored[s], 16 * ((TILES + 1 - s) // 2))

        @block.vector
        def _(dve):
            dve.memset(eps[:, :], EPS).then_inc(eps_set, 1)
            dve.wait_ge(consts, 16 * (NH + 1))
            for k in range(KD):
                dve.wait_ge(w_half, k + 1)
                dve.tensor_tensor(w_lo[:, k, :], w_raw[k % 2][:, :], f(w_hi[:, k, :]), ALU.subtract).then_inc(w_ready, 1)

            def norm(t, s, u):
                dve.wait_ge(squared[s], u + 1)
                dve.wait_ge(logs[s], u)
                dve.tensor_reduce(st[s][:, 0, :], sq[s][:, :, :], AX.X, ALU.add).then_inc(summed[s], 1)
                dve.wait_ge(z_exp[s], u + 1)
                dve.tensor_scalar(ez[s][:, :], ez[s][:, :], 3e38, 1.0, ALU.min, ALU.add).then_inc(z_one, 1)
                dve.wait_ge(z_one, t + 1)
                dve.reciprocal(ez[s][:, :], ez[s][:, :]).then_inc(z_inv[s], 1)
                dve.wait_ge(yg_ready[s], u + 1)
                dve.wait_ge(rooted[s], u + 1)
                dve.wait_ge(turned[s], u)
                dve.tensor_tensor(mix[s][:, :].rearrange("p (h d) -> p h d", d=P), yg[s][:, :, :],
                                  st[s][:, 2, :].unsqueeze(2).to_broadcast([P, NH, P]), ALU.mult).then_inc(mixed[s], 1)

            def lo(t, s, u):
                dve.wait_ge(m_half[s], u + 1)
                dve.tensor_tensor(m_lo[s][:, :, :], pT[:, :, :], f(m_hi[s][:, :, :]), ALU.subtract).then_inc(m_ready[s], 1)

            def u_part(t, s, u):
                dve.wait_ge(u_half[s], u + 1)
                dve.tensor_tensor(u_lo[s][:, :, :], pU[:, :, :], f(u_hi[s][:, :, :]), ALU.subtract).then_inc(u_ready[s], 1)

            def norm2(t, s, u):
                dve.wait_ge(multiplied[s], u + 1)
                if isinstance(t, int) and t == 0:
                    dve.wait_ge(head_loaded, 16)
                dve.wait_ge(res_loaded[s], 16 * (u + 1))
                dve.wait_ge(h2_stored[s], 16 * u)
                dve.tensor_tensor(h2[s][:, :], pP[s][:, :, :].rearrange("p b n -> p (b n)"), res[s][:, :],
                                  ALU.add).then_inc(h2_ready[s], 1)
                dve.wait_ge(h2_root[s], u + 1)
                dve.wait_ge(xn_turned[s], u)
                dve.scalar_tensor_tensor(out=xn[s][:, :], in0=h2[s][:, :], scalar=st2[s][:, 2:3], in1=ffn_gain[:, :],
                                         op0=ALU.mult, op1=ALU.mult).then_inc(xn_ready[s], 1)

            four_tiles(dve, TILES, norm, lo, u_part, norm2)

        @block.tensor
        def _(pe):
            pe.wait_ge(id_made, 2)

            def turn(t, s, u):
                pe.wait_ge(mixed[s], u + 1)
                pe.wait_ge(m_ready[1 - s], u + s)
                for k in range(KD):
                    m = pe.transpose(pT[:, k, :], mix[s][:, k * P:k * P + P], ident[:, :])
                m.then_inc(turned[s], 1)

            def turn2(t, s, u):
                pe.wait_ge(xn_ready[s], u + 1)
                pe.wait_ge(u_ready[1 - s], u + s)
                for k in range(KD):
                    m = pe.transpose(pU[:, k, :], xn[s][:, k * P:k * P + P], ident[:, :])
                m.then_inc(xn_turned[s], 1)

            def multiply(t, s, u):
                if isinstance(t, int) and t == 0:
                    pe.wait_ge(w_ready, KD)
                pe.wait_ge(m_ready[s], u + 1)
                pe.wait_ge(h2_ready[s], u)
                for bank in range(2):
                    for k in range(KD):
                        for n_pass, (a, b) in enumerate(((m_hi, w_hi), (m_hi, w_lo), (m_lo, w_hi))):
                            m = pe.matmul(pP[s][:, bank, :], a[s][:, k, :], b[:, k, bank * 512:bank * 512 + 512],
                                          start=(k == 0 and n_pass == 0), stop=(k == KD - 1 and n_pass == 2))
                m.then_inc(multiplied[s], 1)

            four_tiles(pe, TILES, None, turn, turn2, multiply)


def stage_ffn(nc, A, S):
    with ExitStack() as ctx:
        r = Room(nc, ctx, "ff")
        B = 512
        BLOCKS = SEQ // B
        TT = B // P
        TAPS = 3
        HALO = TAPS - 1
        DOWN = FT
        HS = DOWN // 2
        USES = (FT + DOWN) // 2
        assert FT % 2 == 0 and HS * 2 == FT
        u_hi = r.sb("u_hi", [P, KD, B], F32R)
        u_lo = r.sb("u_lo", [P, KD, B], F32R)
        g_hi = r.sb("g_hi", [P, FT, B], F32R)
        g_lo = r.sb("g_lo", [P, FT, B], F32R)
        w_raw = [r.sb(f"w_raw{i}", [P, 2 * KD * P]) for i in range(2)]
        w_hi = [r.sb(f"w_hi{i}", [P, 2 * KD * P], F32R) for i in range(2)]
        w_lo = [r.sb(f"w_lo{i}", [P, 2 * KD * P], F32R) for i in range(2)]
        ident = r.sb("ident", [P, P])
        taps_in = r.sb("taps_in", [(TAPS + 1) * FT, P])
        taps = r.sb("taps", [P, (TAPS + 1) * FT])
        head_hi = r.sb("head_hi", [P, KD, HALO])
        head_lo = r.sb("head_lo", [P, KD, HALO])
        head = r.sb("head", [P, KD, HALO])
        halo = r.sb("halo", [P, FT, HALO])
        gb = [r.sb(f"gb{i}", [P, HALO + B]) for i in range(2)]
        acc = [r.sb(f"acc{i}", [P, B]) for i in range(2)]
        g = [r.sb(f"g{i}", [P, B]) for i in range(2)]
        yb = r.sb("yb", [P, TT, B])
        pG = [r.ps(f"pG{i}", [P, B]) for i in range(2)]
        pU = [r.ps(f"pU{i}", [P, B]) for i in range(2)]
        pD = [r.ps(f"pD{i}", [P, B]) for i in range(TT)]

        consts, id_made, taps_turned, taps_ready, head_ready = (
            r.sem(x) for x in ("consts", "id_made", "taps_turned", "taps_ready", "head_ready"))
        w_loaded, w_half, w_ready, unit_done = (r.sems(x) for x in ("w_loaded", "w_half", "w_ready", "unit_done"))
        u_loaded, gate_done, gate_out = r.sem("u_loaded"), r.sems("gate_done"), r.sems("gate_out")
        halo_used = r.sems("halo_used")
        conv_step, convolved, active, g_made, g_half, g_ready = (
            r.sem("conv_step"), r.sems("convolved"), r.sems("active"), r.sems("g_made"), r.sems("g_half"), r.sems("g_ready"))
        res_loaded, y_ready, stored = r.sem("res_loaded"), r.sem("y_ready"), r.sem("stored")

        def block_steps(eng, b, split, mid, back, down):
            w0, c0 = b * USES, b * (FT // 2)
            pairs = (FT - 2) // 2

            def step(t, s, u, prev):
                if split:
                    split(*((t + 1, 1 - s, w0 + u + s)))
                if mid:
                    mid(t, s, c0 + u)
                if prev is not None and back:
                    back(*prev)

            if split:
                split(0, 0, w0)
            step(0, 0, 0, None)
            with eng.Fori(0, pairs) as p:
                step(2 * p + 1, 1, p, (2 * p, 0, c0 + p))
                step(2 * p + 2, 0, p + 1, (2 * p + 1, 1, c0 + p))
            step(FT - 1, 1, FT // 2 - 1, (FT - 2, 0, c0 + FT // 2 - 1))
            if back:
                back(FT - 1, 1, c0 + FT // 2 - 1)
            for j in range(DOWN):
                if split and j + 1 < DOWN:
                    n = FT + j + 1
                    split(n, n % 2, w0 + n // 2)
                if down:
                    down(j)

        def all_blocks(eng, run):
            run(0)
            with eng.Fori(1, BLOCKS) as b:
                run(b)

        block = ctx.enter_context(nc.Block())

        @block.sync
        def _(sp):
            sp.dma_start(taps_in[0:TAPS * FT, :], A["ffn_conv_w"][0].rearrange("j (m p) -> (j m) p", p=P)).then_inc(consts, 16)
            sp.dma_start(taps_in[TAPS * FT:, :], A["ffn_conv_b"][0].rearrange("(m p) -> m p", p=P)).then_inc(consts, 16)
            for to, n in ((head_hi, 0), (head_lo, 1)):
                sp.dma_start(to[:, :, :], S["u2T"][n, :, :, N_META - HALO:N_META]).then_inc(consts, 16)

            def load(n, s, u):
                sp.wait_ge(unit_done[s], u)
                sp.wait_ge(consts, 64)
                if isinstance(n, int) and n >= FT:
                    j = n - FT
                    cols = slice(j // HS * 512, j // HS * 512 + 512)
                    for i in range(2):
                        ft = 2 * (j % HS) + i
                        sp.dma_start(w_raw[s][:, i * 512:i * 512 + 512],
                                     A["w_down"][0, ft * P:ft * P + P, cols]).then_inc(w_loaded[s], 16)
                else:
                    for i, name in enumerate(("w_gate", "w_up")):
                        sp.dma_start(w_raw[s][:, i * D:i * D + D].rearrange("p (k n) -> p k n", n=P),
                                     A[name][0].rearrange("(k p) n -> p k n", p=P)[:, :, bass.ds(n * P, P)]
                                     ).then_inc(w_loaded[s], 16)

            all_blocks(sp, lambda b: block_steps(sp, b, load, None, None, None))

        @block.gpsimd
        def _(pool):
            make_identity(pool, ident, id_made)
            for b in range(BLOCKS):
                cols = slice(N_META + b * B, N_META + b * B + B)
                if b == 0:
                    for k in range(KD):
                        pool.dma_start(f(u_hi[:, k, :]), S["u2T"][0, :, k, cols]).then_inc(u_loaded, 16)
                        pool.dma_start(f(u_lo[:, k, :]), S["u2T"][1, :, k, cols]).then_inc(u_loaded, 16)
                for half in range(2):
                    hc = slice(half * 512, half * 512 + 512)
                    if b or half:
                        pool.wait_ge(stored, 16 * (2 * b + half))
                    pool.dma_start(yb[:, :, :], S["h2"][cols, hc].rearrange("(t p) n -> p t n", p=P)).then_inc(res_loaded, 16)
                    if half == 0 and b + 1 < BLOCKS:
                        for s in range(2):
                            pool.wait_ge(unit_done[s], USES * b + FT // 2)
                        nxt = slice(cols.stop, cols.stop + B)
                        for k in range(KD):
                            pool.dma_start(f(u_hi[:, k, :]), S["u2T"][0, :, k, nxt]).then_inc(u_loaded, 16)
                            pool.dma_start(f(u_lo[:, k, :]), S["u2T"][1, :, k, nxt]).then_inc(u_loaded, 16)
                    pool.wait_ge(y_ready, TT * (2 * b + half + 1))
                    pool.dma_start(A["out"][0, b * B:b * B + B, hc].rearrange("(t p) n -> p t n", p=P),
                                   yb[:, :, :]).then_inc(stored, 16)
            pool.wait_ge(stored, 16 * 2 * BLOCKS)

        @block.scalar
        def _(act):
            act.wait_ge(id_made, 2)

            def split(n, s, u):
                w = D if isinstance(n, int) and n >= FT else 2 * D
                act.wait_ge(w_loaded[s], 32 * (u + 1))
                act.wait_ge(unit_done[s], u)
                act.activation(w_hi[s][:, 0:w], w_raw[s][:, 0:w], ACT.Copy).then_inc(w_half[s], 1)

            def run(b):
                def gate(t, s, c):
                    act.wait_ge(gate_done[s], c + 1)
                    act.wait_ge(convolved[s], c)
                    act.activation(gb[s][:, HALO:B], pG[s][:, 0:B - HALO], ACT.Copy)
                    before = pD[s][:, 0:HALO] if isinstance(b, int) else halo[:, bass.ds(t, 1), :].rearrange("p a n -> p (a n)")
                    act.activation(gb[s][:, 0:HALO], before, ACT.Copy).then_inc(halo_used[s], 1)
                    act.wait_ge(halo_used[s], c + 1)
                    act.activation(gb[s][:, B:], pG[s][:, B - HALO:], ACT.Copy)
                    act.activation(halo[:, bass.ds(t, 1), :].rearrange("p a n -> p (a n)"), pG[s][:, B - HALO:], ACT.Copy).then_inc(gate_out[s], 1)

                def silu(t, s, c):
                    act.wait_ge(convolved[s], c + 1)
                    act.activation(acc[s][:, :], acc[s][:, :], ACT.Silu).then_inc(active[s], 1)
                    act.wait_ge(g_made[s], c + 1)
                    act.activation(g_hi[:, bass.ds(t, 1), :].rearrange("p a n -> p (a n)"), g[s][:, :],
                                   ACT.Copy).then_inc(g_half[s], 1)

                block_steps(act, b, split, gate, silu, None)

            all_blocks(act, run)

        @block.vector
        def _(dve):
            dve.wait_ge(taps_turned, 1)
            dve.tensor_copy(taps[:, :], pG[0][:, 0:(TAPS + 1) * FT]).then_inc(taps_ready, 1)
            dve.wait_ge(consts, 64)
            dve.tensor_tensor(head[:, :, :], head_hi[:, :, :], head_lo[:, :, :], ALU.add).then_inc(head_ready, 1)
            dve.wait_ge(taps_ready, 1)

            def split(n, s, u):
                w = D if isinstance(n, int) and n >= FT else 2 * D
                dve.wait_ge(w_half[s], u + 1)
                dve.tensor_tensor(w_lo[s][:, 0:w], w_raw[s][:, 0:w], f(w_hi[s][:, 0:w]), ALU.subtract).then_inc(w_ready[s], 1)

            def run(b):
                def conv(t, s, c):
                    dve.wait_ge(gate_out[s], c + 1)
                    dve.wait_ge(g_made[s], c)
                    n = HALO * (b * FT + t)
                    tap = [taps[:, bass.ds(j * FT + t, 1)] for j in range(TAPS + 1)]
                    dve.tensor_scalar(acc[s][:, :], gb[s][:, HALO:], tap[HALO], tap[TAPS], ALU.mult, ALU.add).then_inc(conv_step, 1)
                    for j in range(HALO):
                        dve.wait_ge(conv_step, n + j + 1)
                        dve.scalar_tensor_tensor(out=acc[s][:, :], in0=gb[s][:, j:j + B], scalar=tap[j], in1=acc[s][:, :],
                                                 op0=ALU.mult, op1=ALU.add).then_inc(conv_step if j < HALO - 1 else convolved[s], 1)

                def glu(t, s, c):
                    dve.wait_ge(active[s], c + 1)
                    dve.wait_ge(unit_done[s], c + b * (USES - FT // 2) + 1)
                    dve.wait_ge(g_ready[s], c)
                    dve.tensor_tensor(g[s][:, :], pU[s][:, :], acc[s][:, :], ALU.mult).then_inc(g_made[s], 1)
                    dve.wait_ge(g_half[s], c + 1)
                    one = bass.ds(t, 1)
                    dve.tensor_tensor(g_lo[:, one, :].rearrange("p a n -> p (a n)"), g[s][:, :],
                                      f(g_hi[:, one, :].rearrange("p a n -> p (a n)")), ALU.subtract).then_inc(g_ready[s], 1)

                def down(j):
                    if j % HS == HS - 1:
                        h = 2 * b + j // HS
                        dve.wait_ge(res_loaded, 16 * (h + 1))
                        dve.wait_ge(unit_done[j % 2], b * USES + (FT + j) // 2 + 1)
                        for t in range(TT):
                            dve.tensor_tensor(yb[:, t, :], pD[t][:, :], yb[:, t, :], ALU.add).then_inc(y_ready, 1)

                block_steps(dve, b, split, conv, glu, down)

            all_blocks(dve, run)

        @block.tensor
        def _(pe):
            pe.wait_ge(id_made, 2)
            pe.wait_ge(consts, 64)
            n = (TAPS + 1) * FT
            pe.transpose(pG[0][:, 0:n], taps_in[:, :], ident[0:n, 0:n]).then_inc(taps_turned, 1)
            pe.wait_ge(taps_ready, 1)
            pe.wait_ge(head_ready, 1)

            def run(b):
                w0 = b * USES

                def gate_up(t, s, c):
                    if isinstance(t, int) and t == 0:
                        pe.wait_ge(u_loaded, 32 * KD * (b + 1))
                    u = c + b * (USES - FT // 2)
                    pe.wait_ge(w_ready[s], u + 1)
                    for i, (bank, free, done) in enumerate(((pG, gate_out, gate_done), (pU, g_made, unit_done))):
                        pe.wait_ge(free[s], c)
                        for k in range(KD):
                            o = i * D + k * P
                            for n_pass, (a, x) in enumerate(((w_hi, u_hi), (w_hi, u_lo), (w_lo, u_hi))):
                                m = pe.matmul(bank[s][:, :], a[s][:, o:o + P], x[:, k, :],
                                              start=(k == 0 and n_pass == 0), stop=(k == KD - 1 and n_pass == 2))
                        if i == 0 and isinstance(b, int):
                            for k in range(KD):
                                m = pe.matmul(pD[s][:, 0:HALO], w_raw[s][:, k * P:k * P + P], head[:, k, :],
                                              start=(k == 0), stop=(k == KD - 1))
                        m.then_inc(done[s], 1)

                def down(j):
                    s, half, first = j % 2, j // HS, 2 * (j % HS)
                    pe.wait_ge(w_ready[s], w0 + (FT + j) // 2 + 1)
                    if j in (0, HS - 1):
                        for i in range(2):
                            pe.wait_ge(g_ready[i], FT // 2 * (b + 1) - (j == 0))
                            if isinstance(b, int):
                                pe.wait_ge(gate_out[i], FT // 2)
                    for i in range(2):
                        ft = first + i
                        for t in range(TT):
                            if ft == 0 and not (isinstance(b, int) and half == 0):
                                pe.wait_ge(y_ready, TT * (2 * b + half) + t - TT + 1)
                            for n_pass, (x, a) in enumerate(((g_hi, w_hi), (g_hi, w_lo), (g_lo, w_hi))):
                                m = pe.matmul(pD[t][:, :], x[:, ft, t * P:t * P + P], a[s][:, i * 512:i * 512 + 512],
                                              start=(ft == 0 and n_pass == 0), stop=(ft == FT - 1 and n_pass == 2))
                    m.then_inc(unit_done[s], 1)

                block_steps(pe, b, None, gate_up, None, down)

            all_blocks(pe, run)


def build(nc, A, S, only=None):
    for name, stage in STAGES:
        if only is None or name in only:
            with nc.cleanup_on_exit():
                stage(nc, A, S)


STAGES = [("project", stage_project), ("qkv", stage_qkv), ("conv", stage_conv), ("gates", stage_gates),
          ("intra", stage_intra), ("scan", stage_scan), ("attention", stage_attention),
          ("out", stage_out), ("ffn", stage_ffn)]
SCRATCH = {
    "uT": (2, P, KD, LP), "tok": (LP, TOKW), "qT": (HEADS, QK, LP), "kT": (HEADS, QK, LP), "v": (HEADS, P, TILES, VD),
    "o_mla": (LP, 512), "dtok": (DT * P, 3 * DNW),
    "gcr": (NC * 2, P), "egl": (P, NC, 2, 2), "sc": (P, 7, NC, 2), "prod": (NC, P, 2, 5, P), "o_dn": (DN_PAD + L, DNW),
    "h2": (LP, D), "u2T": (2, P, KD, LP),
}
_INS = ["x", "meta_tokens", "attn_norm_w", "w_in", "q_a_norm_w", "w_q_b", "kv_a_norm_w", "w_kv_b", "q_norm_w",
        "k_norm_w", "mla_out_norm_w", "dn_conv_w", "dn_A_log", "dn_dt_bias", "dn_out_norm_w", "w_out", "ffn_norm_w",
        "w_gate", "w_up", "ffn_conv_w", "ffn_conv_b", "w_down"]


def rope_tables():
    inv = (np.float32(10000.0) ** (-np.arange(HALF, dtype=np.float32) / np.float32(HALF))).astype(np.float32)
    ang = np.arange(LP, dtype=np.float32)[:, None] * inv[None, :]
    return np.stack([np.cos(ang), np.sin(ang)], 1).astype(np.float32)


def declare(nc, arrays):
    A = {name: nc.dram_tensor(f"in_{name}", arrays[f"in_{name}"].shape, F32, kind="ExternalInput").ap()
         for name in _INS + ["rope"]}
    A["out"] = nc.dram_tensor("out", (1, SEQ, D), F32, kind="ExternalOutput").ap()
    S = {name: nc.dram_tensor(f"scr_{name}", shape, F32, kind="Internal").ap() for name, shape in SCRATCH.items()}
    return A, S


def kernel(**inputs):
    import concourse.bacc as bacc
    from concourse.bass_utils import run_bass_kernel_spmd as run

    nc = bacc.Bacc("TRN2", target_bir_lowering=False, num_devices=1)
    arrays = {f"in_{name}": np.ascontiguousarray(inputs[name]) for name in _INS}
    arrays["in_rope"] = rope_tables()
    build(nc, *declare(nc, arrays))
    r = run(nc, [arrays], core_ids=[0])
    return r.results[0]["out"]
```
